# Optimizing a Trainium2 kernel written in Bass

```python
import math
import jax, jax.numpy as jnp
from jax import lax
import numpy as np

D_MODEL = 1024
BATCH = 1
SEQ = 512
DEPTH = 1

N_MOD = 6
GLA_HEADS = 4
GLA_DK = D_MODEL // 2
GLA_DV = D_MODEL
GLA_HEAD_K = GLA_DK // GLA_HEADS
GLA_HEAD_V = GLA_DV // GLA_HEADS
GLA_LOWRANK = 16
GLA_TAU = 16.0
GLA_CHUNK = 64
DIL_PATTERNS = ((128, 1), (512, 4), (2048, 16))
DIL_GROUPS = len(DIL_PATTERNS)
DIL_HEADS_PER_GROUP = 8
DIL_HEAD_DIM = 64
DIL_HEADS = DIL_GROUPS * DIL_HEADS_PER_GROUP
DIL_WIDTH = DIL_HEADS * DIL_HEAD_DIM
DIL_OUT = DIL_HEADS_PER_GROUP * DIL_HEAD_DIM
DIL_BLOCK = 128
REL_BUCKETS = 32
REL_MAX_DIST = 2048
IN_SPLITS = (GLA_DK, GLA_DK, GLA_DV, GLA_DV, GLA_LOWRANK, DIL_WIDTH, DIL_WIDTH, DIL_WIDTH, D_MODEL, D_MODEL)
IN_COLS = sum(IN_SPLITS)
MOE_GROUPS = 4
MOE_EXPERTS = 8
MOE_TOPK = 2
MOE_FF = D_MODEL // 2
LN_EPS = 1e-5

kernel_name = "hybrid_gla_dilated_attn_hmoe_deepnorm"

def layer_norm(x, g, b):
    xf = x.astype(jnp.float32)
    mu = jnp.mean(xf, -1, keepdims=True)
    var = jnp.mean(jnp.square(xf - mu), -1, keepdims=True)
    return ((xf - mu) * lax.rsqrt(var + LN_EPS) * g + b).astype(x.dtype)

def t5_bucket(dist):
    exact = REL_BUCKETS // 2
    d = jnp.maximum(dist, 1).astype(jnp.float32)
    large = exact + (jnp.log(d / exact) / math.log(REL_MAX_DIST / exact) * (REL_BUCKETS - exact)).astype(jnp.int32)
    large = jnp.minimum(large, REL_BUCKETS - 1)
    return jnp.where(dist < exact, dist, large)

def gla(q, k, v, r, lr, w_gate, b_gate, norm_g):
    B, S, _ = q.shape
    n = S // GLA_CHUNK
    log_a = jax.nn.log_sigmoid((lr @ w_gate + b_gate).astype(jnp.float32)) / GLA_TAU

    def chunks(t, hd):
        return t.reshape(B, n, GLA_CHUNK, GLA_HEADS, hd).transpose(1, 0, 3, 2, 4)

    qc = chunks(q * GLA_HEAD_K ** -0.5, GLA_HEAD_K)
    kc = chunks(k, GLA_HEAD_K)
    vc = chunks(v, GLA_HEAD_V)
    gc = chunks(log_a, GLA_HEAD_K)
    causal = jnp.tril(jnp.ones((GLA_CHUNK, GLA_CHUNK), bool))

    def step(state, inp):
        qi, ki, vi, gi = inp
        b = jnp.cumsum(gi, axis=-2)
        o_inter = jnp.einsum('bhck,bhkv->bhcv', qi * jnp.exp(b), state)
        diff = jnp.where(causal[:, :, None], b[:, :, :, None, :] - b[:, :, None, :, :], -jnp.inf)
        att = jnp.einsum('bhtk,bhtsk,bhsk->bhts', qi, jnp.exp(diff), ki)
        o_intra = jnp.einsum('bhts,bhsv->bhtv', att, vi)
        b_last = b[:, :, -1:, :]
        state = state * jnp.exp(b_last)[:, :, 0, :, None] + jnp.einsum('bhsk,bhsv->bhkv', ki * jnp.exp(b_last - b), vi)
        return state, o_inter + o_intra

    state0 = jnp.zeros((B, GLA_HEADS, GLA_HEAD_K, GLA_HEAD_V), jnp.float32)
    _, o = lax.scan(step, state0, (qc, kc, vc, gc))
    o = o.transpose(1, 0, 3, 2, 4).reshape(B, S, GLA_HEADS, GLA_HEAD_V)
    o = o * lax.rsqrt(jnp.mean(o * o, -1, keepdims=True) + LN_EPS) * norm_g.reshape(GLA_HEADS, GLA_HEAD_V)
    o = o * jax.nn.silu(r.astype(jnp.float32)).reshape(B, S, GLA_HEADS, GLA_HEAD_V)
    return o.reshape(B, S, GLA_DV).astype(q.dtype)

def dilated_group(q, k, v, bias_table, window, dilation):
    B, S, H, Dh = q.shape
    L = S // dilation
    nb = -(-L // DIL_BLOCK)
    Lp = nb * DIL_BLOCK

    def to_blocks(t):
        t = t.reshape(B, L, dilation, H, Dh).transpose(0, 2, 3, 1, 4)
        t = jnp.pad(t, ((0, 0), (0, 0), (0, 0), (0, Lp - L), (0, 0)))
        return t.reshape(B, dilation, H, nb, DIL_BLOCK, Dh)

    def with_prev(t):
        prev = jnp.pad(t, ((0, 0), (0, 0), (0, 0), (1, 0), (0, 0), (0, 0)))[:, :, :, :-1]
        return jnp.concatenate([prev, t], axis=-2)

    qb = to_blocks(q)
    kk = with_prev(to_blocks(k))
    vv = with_prev(to_blocks(v))
    s = jnp.einsum('brhnqe,brhnke->brhnqk', qb, kk).astype(jnp.float32) * Dh ** -0.5
    qi = jnp.arange(DIL_BLOCK)[:, None]
    kj = jnp.arange(2 * DIL_BLOCK)[None, :]
    m = qi + DIL_BLOCK - kj
    n_steps = window // dilation
    band = (m >= 0) & (m <= n_steps)
    key_pos = jnp.arange(nb)[:, None, None] * DIL_BLOCK - DIL_BLOCK + kj[None]
    valid = band[None] & (key_pos >= 0)
    bucket = t5_bucket(jnp.clip(m, 0, n_steps) * dilation)
    bias = jnp.transpose(bias_table[bucket], (2, 0, 1)).astype(jnp.float32)
    s = jnp.where(valid, s + bias[:, None], -jnp.inf)
    mx = jnp.max(s, axis=-1, keepdims=True)
    p = jnp.exp(s - mx)
    den = jnp.sum(p, axis=-1, keepdims=True)
    o = jnp.einsum('brhnqk,brhnke->brhnqe', p / den, vv)
    lse = (mx + jnp.log(den))[..., 0]
    o = o.reshape(B, dilation, H, Lp, Dh)[:, :, :, :L].transpose(0, 3, 1, 2, 4).reshape(B, S, H, Dh)
    lse = lse.reshape(B, dilation, H, Lp)[..., :L].transpose(0, 3, 1, 2).reshape(B, S, H)
    return o, lse

def dilated_attention(q, k, v, rel_bias):
    B, S = q.shape[:2]
    outs, lses = [], []
    for g, (window, dilation) in enumerate(DIL_PATTERNS):
        table = rel_bias[:, g * DIL_HEADS_PER_GROUP:(g + 1) * DIL_HEADS_PER_GROUP]
        o, lse = dilated_group(q[:, :, g], k[:, :, g], v[:, :, g], table, window, dilation)
        outs.append(o)
        lses.append(lse)
    wts = jax.nn.softmax(jnp.stack(lses), axis=0)
    out = jnp.einsum('gbsh,gbshe->bshe', wts, jnp.stack(outs))
    return out.reshape(B, S, DIL_OUT).astype(q.dtype)

def mixer_sublayer(u, w_in, w_gla_gate, b_gla_gate, gla_norm, w_proj_gla, w_proj_attn, w_out, rel_bias):
    B, S, _ = u.shape
    z = u @ w_in
    cuts = np.cumsum(IN_SPLITS)[:-1].tolist()
    qa, ka, va, ra, lra, qd, kd, vd, ga, gd = jnp.split(z, cuts, axis=-1)
    y_gla = gla(qa, ka, va, ra, lra, w_gla_gate, b_gla_gate, gla_norm)
    hs = (B, S, DIL_GROUPS, DIL_HEADS_PER_GROUP, DIL_HEAD_DIM)
    y_att = dilated_attention(qd.reshape(hs), kd.reshape(hs), vd.reshape(hs), rel_bias)
    merged = jax.nn.sigmoid(ga) * (y_gla @ w_proj_gla) + jax.nn.sigmoid(gd) * (y_att @ w_proj_attn)
    return merged @ w_out

def hier_moe(u, w_rg, b_rg, w_re, b_re, w_gate, w_up, w_down):
    B, S, D = u.shape
    xf = u.reshape(-1, D)
    N = xf.shape[0]
    g_logits = (xf @ w_rg + b_rg).astype(jnp.float32)
    g_prob = jax.nn.softmax(g_logits, -1)
    g_val, g_idx = lax.top_k(g_prob, 1)
    e_logits = (xf @ w_re + b_re).astype(jnp.float32).reshape(N, MOE_GROUPS, MOE_EXPERTS)
    e_in = jnp.take_along_axis(e_logits, g_idx[:, :, None], axis=1)[:, 0]
    top_v, top_i = lax.top_k(e_in, MOE_TOPK)
    top_w = jax.nn.softmax(top_v, -1)
    e_w = jnp.sum(jax.nn.one_hot(top_i, MOE_EXPERTS, dtype=jnp.float32) * top_w[..., None], axis=1)
    combine = jax.nn.one_hot(g_idx[:, 0], MOE_GROUPS, dtype=jnp.float32)[:, :, None] * (g_val * e_w)[:, None, :]
    out = jnp.zeros((N, D), jnp.float32)
    for g in range(MOE_GROUPS):
        h = jax.nn.silu(jnp.einsum('nd,edf->nef', xf, w_gate[g])) * jnp.einsum('nd,edf->nef', xf, w_up[g])
        out = out + jnp.einsum('nef,ne,efd->nd', h, combine[:, g], w_down[g])
    return out.reshape(B, S, D).astype(u.dtype)

def setup_inputs(seed: int = 0) -> dict:
    key = jax.random.key(seed)
    ks = jax.random.split(key, 24)
    beta = (8.0 * DEPTH) ** -0.25
    f32 = jnp.float32

    def nrm(k, shape, scale):
        return jax.random.normal(k, shape, f32) * scale

    starts = np.concatenate([[0], np.cumsum(IN_SPLITS)])
    col_scale = np.ones(IN_COLS, np.float32)
    col_scale[starts[2]:starts[3]] = beta
    col_scale[starts[7]:starts[8]] = beta
    Ld = DEPTH
    return {
        "x": nrm(ks[0], (BATCH, SEQ, D_MODEL), 1.0),
        "c": nrm(ks[1], (BATCH, D_MODEL), 1.0),
        "rel_bias": nrm(ks[2], (REL_BUCKETS, DIL_HEADS), 0.1),
        "w_ada": nrm(ks[3], (Ld, D_MODEL, N_MOD * D_MODEL), D_MODEL ** -0.5),
        "b_ada": nrm(ks[4], (Ld, N_MOD * D_MODEL), 0.02),
        "w_in": nrm(ks[5], (Ld, D_MODEL, IN_COLS), D_MODEL ** -0.5) * jnp.asarray(col_scale),
        "w_gla_gate": nrm(ks[6], (Ld, GLA_LOWRANK, GLA_DK), GLA_LOWRANK ** -0.5),
        "b_gla_gate": nrm(ks[7], (Ld, GLA_DK), 0.1),
        "gla_norm": 1.0 + nrm(ks[8], (Ld, GLA_DV), 0.02),
        "w_proj_gla": nrm(ks[9], (Ld, GLA_DV, D_MODEL), GLA_DV ** -0.5 * beta),
        "w_proj_attn": nrm(ks[10], (Ld, DIL_OUT, D_MODEL), DIL_OUT ** -0.5 * beta),
        "w_out": nrm(ks[11], (Ld, D_MODEL, D_MODEL), D_MODEL ** -0.5 * beta),
        "ln1_g": 1.0 + nrm(ks[12], (Ld, D_MODEL), 0.02),
        "ln1_b": nrm(ks[13], (Ld, D_MODEL), 0.02),
        "w_router_group": nrm(ks[14], (Ld, D_MODEL, MOE_GROUPS), D_MODEL ** -0.5),
        "b_router_group": nrm(ks[15], (Ld, MOE_GROUPS), 0.01),
        "w_router_expert": nrm(ks[16], (Ld, D_MODEL, MOE_GROUPS * MOE_EXPERTS), D_MODEL ** -0.5),
        "b_router_expert": nrm(ks[17], (Ld, MOE_GROUPS * MOE_EXPERTS), 0.01),
        "w_exp_gate": nrm(ks[18], (Ld, MOE_GROUPS, MOE_EXPERTS, D_MODEL, MOE_FF), D_MODEL ** -0.5),
        "w_exp_up": nrm(ks[19], (Ld, MOE_GROUPS, MOE_EXPERTS, D_MODEL, MOE_FF), D_MODEL ** -0.5 * beta),
        "w_exp_down": nrm(ks[20], (Ld, MOE_GROUPS, MOE_EXPERTS, MOE_FF, D_MODEL), MOE_FF ** -0.5 * beta),
        "ln2_g": 1.0 + nrm(ks[21], (Ld, D_MODEL), 0.02),
        "ln2_b": nrm(ks[22], (Ld, D_MODEL), 0.02),
    }

def reference(x, c, rel_bias, w_ada, b_ada, w_in, w_gla_gate, b_gla_gate, gla_norm, w_proj_gla, w_proj_attn,
              w_out, ln1_g, ln1_b, w_router_group, b_router_group, w_router_expert, b_router_expert,
              w_exp_gate, w_exp_up, w_exp_down, ln2_g, ln2_b):
    alpha = (2.0 * DEPTH) ** 0.25
    for l in range(DEPTH):
        mods = jax.nn.silu(c) @ w_ada[l] + b_ada[l]
        sh1, sc1, g1, sh2, sc2, g2 = [m[:, None, :] for m in jnp.split(mods, N_MOD, axis=-1)]
        u = x * (1.0 + sc1) + sh1
        y = mixer_sublayer(u, w_in[l], w_gla_gate[l], b_gla_gate[l], gla_norm[l], w_proj_gla[l],
                           w_proj_attn[l], w_out[l], rel_bias)
        x = layer_norm(alpha * x + g1 * y, ln1_g[l], ln1_b[l])
        u = x * (1.0 + sc2) + sh2
        y = hier_moe(u, w_router_group[l], b_router_group[l], w_router_expert[l], b_router_expert[l],
                     w_exp_gate[l], w_exp_up[l], w_exp_down[l])
        x = layer_norm(alpha * x + g2 * y, ln2_g[l], ln2_b[l])
    return x


_drawn_inputs = setup_inputs


def setup_inputs(seed=0):
    import zlib

    import numpy as np

    out = dict(_drawn_inputs(seed))
    spreads = {}
    factors = {'rel_bias': 106.578,
     'b_ada': 3.659,
     'b_gla_gate': 7.172,
     'gla_norm': 94.371,
     'b_router_group': 200.0,
     'b_router_expert': 32.228,
     'ln2_g': 20.763,
     'ln2_b': 21.341,
     'w_proj_attn': 2.899,
     'ln1_g': 2.69}
    for name, (base, spread) in spreads.items():
        noise = np.random.default_rng([zlib.crc32(name.encode()), seed]).standard_normal(out[name].shape)
        drawn = base * np.exp(spread * noise) if base else spread * noise
        out[name] = __import__('jax').numpy.asarray(drawn.astype(out[name].dtype))
    for name, factor in factors.items():
        out[name] = (out[name] * factor).astype(out[name].dtype)
    return out
```

```python
import concourse.bass as bass
from concourse import mybir
from contextlib import ExitStack
import math
import numpy as np

P = 128
D = 1024
S = 512
KD = D // P
NT = S // P
N_MOD = 6
GH, GDK, GDV = 4, 128, 256
CHUNK, SUB = 64, 16
NCH, NSUB = S // CHUNK, CHUNK // SUB
LOWRANK, TAU = 16, 16.0
GROUPS, HPG, DH = 3, 8, 64
STEP = (1, 4, 4)
BUCKETS, MAX_DIST = 32, 2048
MASKED = -1.0e30
EPS = 1e-5
ALPHA = 2.0 ** 0.25
EG, EPG = 4, 8
NE = EG * EPG
FF = D // 2
C = 128
MAX_EXTRA = 8
NCHUNK = NE + MAX_EXTRA + 1
CLAMP = 40.0

QA, KA, VA, RA = 0, 512, 1024, 2048
LRA = 3072
QD = LRA + LOWRANK
KDL, VD = QD + 1536, QD + 3072
GA = VD + 1536
GD = GA + D

IDENT, ONES, TRI, GMASK, RESET, FIRST4, FIRST32, E128, J8, EVEN, TOKID, I32 = np.cumsum(
    [0, 128, 128, 128, 64, 512, 4, 32, 32, 8, 4, 4]).tolist()
NCONST = I32 + 32
JB = (384, 256, 256)
JOFF = (0, 384, 640)
NJ = 896


def shape_constants():
    c = np.zeros((P, NCONST), np.float32)
    p = np.arange(P)[:, None]
    c[:, IDENT:IDENT + P] = np.eye(P)
    c[:, ONES:ONES + P] = 1.0
    c[:, TRI:TRI + P] = p < np.arange(P)[None, :]
    c[:, GMASK:GMASK + CHUNK] = (p % CHUNK) <= np.arange(CHUNK)[None, :]
    c[:, RESET:RESET + S] = (np.arange(S) % CHUNK != 0)
    c[:, FIRST4:FIRST4 + 4] = 4 - np.arange(4)
    c[:, FIRST32:FIRST32 + 32] = 32 - np.arange(32)
    c[:, E128:E128 + 32] = C * np.arange(32)
    c[:, J8:J8 + 8] = np.arange(8)
    c[:, EVEN:EVEN + 4] = 2 * np.arange(4)
    c[:, TOKID:TOKID + 4] = p + P * np.arange(4)
    c[:, I32:I32 + 32] = np.arange(32)
    return c


def t5_bucket(dist):
    exact = BUCKETS // 2
    d = np.maximum(dist, 1).astype(np.float32)
    big = exact + (np.log(d / np.float32(exact)) / np.float32(math.log(MAX_DIST / exact))
                   * np.float32(BUCKETS - exact)).astype(np.int32)
    return np.where(dist < exact, dist, np.minimum(big, BUCKETS - 1))


def bias_selectors():
    sel = np.zeros((BUCKETS + 1, NJ), np.float32)
    for g, (first, last, unit, every) in enumerate(((255, 128, 1, 1), (127, 127, 4, 1), (127, 127, 4, 4))):
        for j in range(JB[g]):
            m = first - j
            if 0 <= m <= last and m % every == 0:
                sel[t5_bucket(np.array(m * unit)), JOFF[g] + j] = 1.0
            else:
                sel[BUCKETS, JOFF[g] + j] = MASKED
    return sel


def build(nc, x, c_col, rel_bias, w_ada, b_ada, w_in, w_gla_gate, b_gla, gla_norm, w_pg, w_pa, w_out,
          ln1_g, ln1_b, w_router, b_router, w_gate, w_up, w_down, ln2_g, ln2_b, const, bias_sel, out):
    f32, u32 = mybir.dt.float32, mybir.dt.uint32
    ALU, ACT, AX = mybir.AluOpType, mybir.ActivationFunctionType, mybir.AxisListType
    ctx = ExitStack()
    BASE = 16512

    def at(name, kb, shape, dt=f32):
        return nc.alloc_sbuf_tensor_at(name, shape, dt, offset=BASE + int(kb * 1024))

    def sem(name):
        return ctx.enter_context(nc.semaphore(name))

    def dram(name, shape, dt=f32):
        return nc.dram_tensor(name, shape, dt, kind="Internal").ap()

    uT = at("uT", 0, [P, KD, S])
    mT = at("mT", 0, [P, KD, S])
    ring = [at(f"ring{i}", 16 + 16 * i, [P, 8, 512]) for i in range(2)]
    qaT = at("qaT", 48, [P, GH, S])
    kaT = at("kaT", 56, [P, GH, S])
    yglaT = at("yglaT", 48, [P, KD, S])
    u2 = at("u2", 48, [P, NT, D])
    x_in = at("x_in", 64, [P, NT, D])
    va = at("va", 64, [P, NT, D])
    sga = at("sga", 64, [P, KD, S])
    u2T = at("u2T", 64, [P, KD, S])
    u_nat = at("u_nat", 80, [P, NT, D])
    sr = at("sr", 80, [P, NT, D])
    sgd = at("sgd", 80, [P, KD, S])
    qg = [at(f"qg{i}", 96 + 24 * i, [P, 4, S]) for i in range(2)]
    kg = [at(f"kg{i}", 104 + 24 * i, [P, 4, S]) for i in range(2)]
    vg = [at(f"vg{i}", 112 + 24 * i, [P, NT, 512]) for i in range(2)]
    x1 = at("x1", 96, [P, NT, D])
    mods = at("mods", 120, [P, 4, D])
    mods_a = at("mods_a", 120, [P, 2, D])
    acc = [at(f"acc{i}", 136 + 2 * i, [P, 512]) for i in range(2)]
    bpad = [at(f"bpad{i}", 140 + 2 * i, [P, 512]) for i in range(2)]
    t1 = at("t1", 144, [P, S])
    t2 = at("t2", 146, [P, S])
    t3 = at("t3", 148, [P, S])
    Bc = at("Bc", 150, [P, S])
    KI = at("KI", 152, [P, NCH, NSUB, CHUNK])
    St = at("St", 160, [P, NCH, GDV])
    gn_b = at("gn_b", 160, [P, D])
    kdN = at("kdN", 168, [P, NT, P])
    attT = at("attT", 170, [P, NT, CHUNK])
    sq_junk = at("sq_junk", 171, [P, GDV])
    sig_t = at("sig_t", 144, [P, 512])
    Ssb = [at(f"Ssb{i}", 144 + 12 * i, [P, 4, 256]) for i in range(2)]
    Pr = [at(f"Pr{i}", 148 + 12 * i, [P, 4, 256]) for i in range(2)]
    PT = [at(f"PT{i}", 152 + 12 * i, [P, 8, P]) for i in range(2)]
    OW = DH + 2
    Og = [at(f"Og{i}", 173 + 8.25 * i, [P, NT, HPG, OW]) for i in range(2)]
    bias = at("bias", 189.5, [P, HPG, 256])
    bvec_sb = at("bvec_sb", 144, [HPG, NJ])
    bsel_sb = at("bsel_sb", 148, [BUCKETS + 1, NJ])
    relb = at("relb", 151.75, [BUCKETS + 1, GROUPS * HPG])
    O1 = at("O1", 144, [P, NT, HPG, OW])
    O2 = at("O2", 152.25, [P, NT, HPG, OW])
    cmb = at("cmb", 160.5, [P, 8, 32])
    yatt = at("yatt", 161.5, [P, NT, HPG, DH])
    yattT = at("yattT", 189.5, [P, 4, S])
    ln_g = at("ln_g", 144, [P, D])
    ln_b = at("ln_b", 148, [P, D])
    lnt = [at(f"lnt{i}", 152 + 4 * i, [P, D]) for i in range(2)]
    wg = [at(f"wg{i}", 48 * i, [P, KD, FF]) for i in range(2)]
    wu = [at(f"wu{i}", 48 * i + 16, [P, KD, FF]) for i in range(2)]
    wd = [at(f"wd{i}", 48 * i + 32, [P, FF // P, D]) for i in range(2)]
    xg = [at(f"xg{i}", 144 + 4 * i, [P, D]) for i in range(2)]
    xT = [at(f"xT{i}", 152 + 4 * i, [P, KD, C]) for i in range(2)]
    sgb = at("sgb", 160, [P, FF])
    gsb = at("gsb", 162, [P, FF])
    hb = at("hb", 164, [P, FF])
    hT = at("hT", 166, [P, FF // P, C])
    yb = [at(f"yb{i}", 168 + 4 * i, [P, D]) for i in range(2)]
    ya = [at(f"ya{i}", 0 + 4 * i, [P, D]) for i in range(2)]
    yc = [at(f"yc{i}", 8 + 4 * i, [P, D]) for i in range(2)]
    r2 = [at(f"r2{i}", 16 + 4 * i, [P, D]) for i in range(2)]
    ln2gb = at("ln2gb", 24, [P, 2, D])
    cst = at("cst", 197.5, [P, NCONST])
    lraT = at("lraT", 202, [LOWRANK, S])
    wgg = at("wgg", 204, [LOWRANK, 512])
    rt_mask = at("rt_mask", 112, [P, 2, NT, NE])
    rt = at("rt", 113, [P, 10, NT, NE])
    rt_w = at("rt_w", 118, [P, 64])
    idsq = at("idsq", 118.5, [NCHUNK, P])
    lra_w = at("lra_w", 96, [P, KD, LOWRANK])
    wr_sb = at("wr_sb", 196.25, [P, KD, EG + NE])
    sm = at("sm", 206, [P, 192])
    csil, ccol = sm[:, 0:8], sm[:, 8:16]
    bgl = sm[:, 16:20]
    Dl = sm[:, 20:28]
    ssq, rstd = sm[:, 28:32], sm[:, 32:36]
    nmx = [sm[:, 36:40], sm[:, 40:44]]
    brt = sm[:, 44:80]
    bnst, bnag = sm[:, 80:92], sm[:, 92:94]
    lrs = sm[:, 94:95]
    ctab_f = sm[:, 96:96 + 48]
    slot_w = sm[:, 144:152]
    rs_t = sm[:, 152:156]
    ui = at("ui", 206.75, [P, 64], u32)
    slot_u = ui[:, 0:8]
    idx_u = ui[:, 8:8 + 48]
    idxc = [ui[:, 56:57], ui[:, 58:59]]
    tab_u = at("tab_u", 119.25, [P, 48], u32)

    ident = cst[:, IDENT:IDENT + P]
    ones = cst[:, ONES:ONES + P]

    ps = ctx.enter_context(nc.psum_tensor("ps", [P, 8, 512], f32))

    def bank(i):
        return ps[:, i, :]

    bvec_d = dram("bvec_d", [HPG, NJ])
    brep_d = [dram(f"brep_d{g}", [P, HPG * JB[g]]) for g in range(GROUPS)]
    att_d = [dram(f"att_d{g}", [S, HPG * OW]) for g in range(2)]
    u2_d = dram("u2_d", [S, D])
    ids_d = dram("ids_d", [NCHUNK * C, 1])
    y_d = dram("y_d", [(NCHUNK - 1) * C, D])

    def cols(w, c0, n=512):
        return w[:, c0:c0 + n].rearrange("(k p) n -> p k n", p=P)

    items = []

    def ada(b):
        items.append(("dve", cols(w_ada, 512 * b), ("ada", b)))

    def zblk(name, c0):
        items.append(("pe", cols(w_in, c0), (name, c0)))

    for b in range(4):
        ada(b)
    zblk("qa", QA), zblk("ka", KA)
    zblk("va", VA), zblk("va", VA + 512), zblk("ra", RA), zblk("ra", RA + 512)
    for g in range(GROUPS):
        zblk("qd", QD + 512 * g), zblk("kd", KDL + 512 * g), zblk("vd", VD + 512 * g)
    for n, c0 in enumerate((GA, GA + 512, GD, GD + 512)):
        zblk("ga" if n < 2 else "gd", c0)
        ada(4 + 2 * n), ada(5 + 2 * n)
    items.append(("pe", cols(w_pg, 0), ("pg", 0)))
    items.append(("pe", cols(w_pg, 512), ("pg", 512)))
    items.append(("pe", w_pa.rearrange("(k p) n -> p k n", p=P), ("pa", 0)))
    items.append(("pe", cols(w_out, 0), ("wo", 0)))
    items.append(("pe", cols(w_out, 512), ("wo", 512)))
    dve_rank = {}
    for n, it in enumerate(items):
        if it[0] == "dve":
            dve_rank[n] = len(dve_rank)
    ada_item = {it[2][1]: n for n, it in enumerate(items) if it[2][0] == "ada"}

    outs = [("uT", k, None) for k in range(KD)]
    steps = [("ada", b) for b in range(4)] + [("z", n) for n in range(KD)]

    def z(o):
        outs.append(o)
        steps.append(("z", len(outs) - 1))

    def block_outs(n, kind):
        return [(kind, q, n) for q in range(4)]

    queue = []
    for n, it in enumerate(items):
        if it[0] == "pe" and it[2][0] in ("qa", "ka", "va", "ra", "qd", "kd", "vd", "ga", "gd"):
            queue.append(block_outs(n, it[2][0]))
    gla_q, att_q, gate_q = queue[:6], queue[6:15], queue[15:]
    z(("lra", 0, None))
    for o in sum(gla_q, []):
        z(o)
    g0 = sum(att_q[0:3], [])
    for h in range(GH):
        z(("gp", h, None))
        steps.append(("gla_args", h))
        z(g0[3 * h]), z(g0[3 * h + 1])
        steps.append(("gla_kt", h))
        steps.append(("gla_kv", h))
        z(g0[3 * h + 2])
        steps.append(("gla_o", h))
    for k in range(KD):
        z(("yT", k, None))
    for g in range(2):
        zs = sum(att_q[3 * g + 3:3 * g + 6], [])
        for j in range(HPG):
            a = g * HPG + j
            if a and j == 0:
                steps.append(("PV", a - 1))
            steps.append(("S", a))
            z(zs.pop(0))
            steps.append(("T", a))
            if j:
                steps.append(("PV", a - 1))
            if j % 2:
                z(zs.pop(0))
    zs, aq = sum(gate_q, []), list(range(4, 12))
    for j in range(HPG):
        a = 2 * HPG + j
        if j == 0:
            steps.append(("PV", a - 1))
            z(zs.pop(0))
        steps.append(("S", a))
        if j:
            z(zs.pop(0))
        steps.append(("T", a))
        if j:
            steps.append(("PV", a - 1))
        z(zs.pop(0))
        if j % 2:
            steps.append(("ada", aq.pop(0))), steps.append(("ada", aq.pop(0)))
    steps.append(("PV", 3 * HPG - 1))
    pgn = [n for n, it in enumerate(items) if it[2][0] == "pg"]
    pan = [n for n, it in enumerate(items) if it[2][0] == "pa"][0]
    won = [n for n, it in enumerate(items) if it[2][0] == "wo"]
    for ct in range(KD):
        z(("pg", ct, pgn[ct // 4]))
    steps.append(("combine", 0))
    for t in range(4):
        z(("yattT", t, None))
    for ct in range(KD):
        z(("pa", ct, pan))
    steps.append(("xload", 0))
    for t in range(NT):
        for half in range(2):
            z(("wo", 2 * t + half, won[half]))
    LAST = {}
    for i, o in enumerate(outs):
        if o[2] is not None:
            LAST[o[2]] = i
    DVE_OUT = ("ra", "gp", "pg", "pa", "wo")

    def freed(i):
        e = outs[i][0] in DVE_OUT
        return e, sum((o[0] in DVE_OUT) == e for o in outs[:i + 1])

    ring_in = [sem(f"ring_in{i}") for i in range(2)]
    ring_dve = sem("ring_used_by_dve")
    small_in, x_load, gn_in, lraw_in, bpad_in = sem("small_in"), sem("x_load"), sem("gn_in"), sem("lraw_in"), [sem("bpad_in0"), sem("bpad_in1")]
    ada_sum, ada_ps, ada_out, bpad_use = sem("ada_sum"), sem("ada_ps"), sem("ada_out"), sem("bpad_used")
    csil_act, csil_rdy = sem("csil_act"), sem("csil_rdy")
    u_rdy = sem("u_rdy")
    out_rdy, out_act, out_dve, sig_rdy = sem("out_rdy"), sem("out_freed_act"), sem("out_freed_dve"), sem("sig_rdy")
    bias_ps, bvec_rdy, bvec_out, bias_in, bias_use = sem("bias_ps"), sem("bvec_rdy"), sem("bvec_out"), sem("bias_in"), sem("bias_used")
    bsel_in, brep_in = sem("bsel_in"), sem("brep_in")
    relb_one = sem("relb_one")
    gla_abs, gla_ln, gla_arg, gla_exp, gla_fac = sem("gla_abs"), sem("gla_ln"), sem("gla_arg"), sem("gla_exp"), sem("gla_fac")
    kt_ps, kt_sb, kv_ps, at_ps, st_sb, at_sb, o_ps, ssq_rdy, y_rdy = (sem(n) for n in (
        "kt_ps", "kt_sb", "kv_ps", "gatt_ps", "state_sb", "gatt_sb", "gla_o_ps", "ssq_rdy", "gla_y"))
    s_ps, s_sb, p_sb, pt_ps, pt_sb, pv_ps, og_rdy = (sem(n) for n in (
        "s_ps", "s_sb", "p_sb", "pt_ps", "pt_sb", "pv_ps", "og_rdy"))
    att_st = [sem("att_store0"), sem("att_store1")]
    att_ld, cm_m, cm_e, yatt_rdy, x1_in = sem("att_load"), sem("cm_max"), sem("cm_exp"), sem("yatt_rdy"), sem("x1_in")
    res_rdy, ln_in, u2_rdy, u2_st, u2T_ps, u2T_sb, lg_ps = (sem(n) for n in (
        "res_rdy", "ln_in", "u2_rdy", "u2_store", "u2T_ps", "u2T_sb", "logits_ps"))
    rt_ge, rt_gexp, rt_asg, rk_ps, slot_rdy, zero_rdy, ids_zero, ids_st, ids_ld, ids_ps, idx_rdy, tab_rdy = (sem(n) for n in (
        "rt_gargs", "rt_gexp", "rt_assign", "rank_ps", "slot_rdy", "zero_rdy", "ids_zero", "ids_store", "ids_load", "ids_ps", "idx_rdy", "tab_rdy"))
    wgi, wui, wdi = ([sem(f"{n}{i}") for i in range(2)] for n in ("w_gate_in", "w_up_in", "w_down_in"))
    xg_in = [sem("xg_in0"), sem("xg_in1")]
    idxc_rdy, m_xt, m_xT, m_gate, m_sig, m_gs, m_up, m_h, m_hps, m_hT, m_y0, m_y, m_ya, m_yd = (sem(n) for n in (
        "idxc_rdy", "moe_xt_ps", "moe_xT_sb", "moe_gate_ps", "moe_sig", "moe_gs", "moe_up_ps", "moe_h",
        "moe_ht_ps", "moe_hT_sb", "moe_y0_ps", "moe_y_ps", "moe_y_act", "moe_y_dve"))
    idxc_seen, y_zero = sem("idxc_seen"), sem("y_zero")
    y_st = [sem("y_store0"), sem("y_store1")]
    fin_in = [sem("fin_in0"), sem("fin_in1")]
    fin_use, fin_rdy, ln2_in = sem("fin_used"), sem("fin_rdy"), sem("ln2_in")
    out_st = [sem("out_store0"), sem("out_store1")]
    dve_own, act_own, pool_own = sem("dve_own"), sem("act_own"), sem("pool_own")

    own = {"dve": 0, "act": 0, "pool": 0}

    def kv_bank(c):
        half = GDV * (c // 2 % 2)
        return ps[:, 2 + 2 * (c % 2) + c // 4, half:half + GDV]

    def wait(eng, s, v):
        if not isinstance(v, int) or v > 0:
            eng.wait_ge(s, v)

    def freed_wait(pe, i):
        if i >= 2:
            e, v = freed(i - 2)
            pe.wait_ge(out_dve if e else out_act, v)

    def perm_in(v, g):
        r = STEP[g]
        return v if r == 1 else v.rearrange("p (l r) -> p r l", r=r)

    def perm_out(v, g):
        r = STEP[g]
        return v if r == 1 else v.rearrange("p (r l) -> p r l", r=r)

    def token_tile(k, g, t):
        if g == 0:
            return uT[:, k, P * t:P * t + P]
        return uT[:, k, :].rearrange("p (l r) -> p r l", r=4)[:, t, :]

    def group_of(n):
        c0 = items[n][2][1]
        return (c0 - QD) % 1536 // 512

    def pair_count(eng):
        return eng.value_load(tab_u[0:1, NCHUNK:NCHUNK + 1], min_val=NE // 2, max_val=(NE + MAX_EXTRA) // 2)

    block = ctx.enter_context(nc.Block())

    @block.sync
    def _(sp):
        sp.dma_start(ccol, c_col).then_inc(small_in, 16)
        sp.dma_start(cst[:, :], const).then_inc(small_in, 16)
        sp.dma_start(bgl, b_gla).then_inc(small_in, 16)
        sp.dma_start(wgg[:, :], w_gla_gate).then_inc(small_in, 16)
        sp.dma_start(brt, b_router.unsqueeze(0).broadcast_to([P, EG + NE])).then_inc(small_in, 16)

        def item(n):
            if n >= 2:
                m = n - 2
                if items[m][0] == "dve":
                    sp.wait_ge(ring_dve, dve_rank[m] + 1)
                else:
                    sp.wait_ge(out_rdy, LAST[m] + 1)
            kind = items[n][2][0]
            dst = ring[n % 2][:, :, :]
            if kind == "pa":
                dst = dst.rearrange("p (k a) n -> p k (a n)", a=2)
            if kind == "ada":
                b = items[n][2][1]
                if b >= 2:
                    sp.wait_ge(bpad_use, b - 1)
                if b == 4:
                    sp.wait_ge(pv_ps, 2 * HPG)
                sp.wait_ge(zero_rdy, 1 if b < 4 else 2)
                sp.dma_start(bpad[b % 2][0:1, :], b_ada[:, 512 * b:512 * b + 512]).then_inc(bpad_in[b % 2], 16)
            sp.dma_start(dst, items[n][1]).then_inc(ring_in[n % 2], 16)

        n_items = len(items)
        for n in range(n_items):
            item(n)
            if n == 1:
                sp.dma_start(x_in[:, :, :], x.rearrange("(t p) d -> p t d", p=P)).then_inc(x_load, 16)
                sp.dma_start(lra_w[:, :, :], cols(w_in, LRA, LOWRANK)).then_inc(lraw_in, 16)
                sp.dma_start(gn_b[:, :], gla_norm.broadcast_to([P, D])).then_inc(gn_in, 16)
        sp.wait_ge(out_rdy, len(outs))
        for s in range(2):
            if s == 1:
                sp.wait_ge(lg_ps, 1)
                sp.wait_ge(u2_st, 16 * NT)
            sp.dma_start(wg[s][:, :, :], w_gate[s].rearrange("(k p) n -> p k n", p=P)).then_inc(wgi[s], 16)
            sp.dma_start(wu[s][:, :, :], w_up[s].rearrange("(k p) n -> p k n", p=P)).then_inc(wui[s], 16)
            sp.dma_start(wd[s][:, :, :], w_down[s].rearrange("(k p) n -> p k n", p=P)).then_inc(wdi[s], 16)
        sp.wait_ge(tab_rdy, 1)
        with sp.Fori(1, pair_count(sp)) as i:
            for s in range(2):
                e = sp.value_load(tab_u[0:1, bass.ds(2 * i + s, 1)], min_val=0, max_val=NE - 1)
                sp.wait_ge(m_gate, 2 * i + s - 1)
                sp.dma_start(wg[s][:, :, :], w_gate[bass.ds(e, 1)].rearrange("e (k p) n -> p (e k) n", p=P)).then_inc(wgi[s], 16)
                sp.wait_ge(m_up, 2 * i + s - 1)
                sp.dma_start(wu[s][:, :, :], w_up[bass.ds(e, 1)].rearrange("e (k p) n -> p (e k) n", p=P)).then_inc(wui[s], 16)
                sp.wait_ge(m_y, 2 * i + s - 1)
                sp.dma_start(wd[s][:, :, :], w_down[bass.ds(e, 1)].rearrange("e (k p) n -> p (e k) n", p=P)).then_inc(wdi[s], 16)

    @block.gpsimd
    def _(pool):
        def link(ins):
            own["pool"] += 1
            ins.then_inc(pool_own, 1)
            pool.wait_ge(pool_own, own["pool"])

        link(pool.memset(bpad[0][:, :], 0.0))
        link(pool.memset(bpad[1][:, :], 0.0))
        link(pool.memset(idsq[:, :], 0.0))
        link(pool.memset(relb[BUCKETS:BUCKETS + 1, :], 1.0))
        pool.sem_inc(relb_one, 1)
        pool.sem_inc(zero_rdy, 1)
        pool.dma_start(ids_d.rearrange("(i p) o -> i (p o)", p=P), idsq[:, :]).then_inc(ids_zero, 16)
        kz = KI[:, :, :, :].rearrange("p c i s -> p (c i s)")
        link(pool.memset(kz, 0.0))
        pool.dma_start(y_d[NE * C:(NE + MAX_EXTRA) * C, :].rearrange("(p i) d -> p (i d)", p=P)
                       .rearrange("p (a b) -> p a b", b=2048),
                       kz.unsqueeze(1).broadcast_to([P, MAX_EXTRA * D // 2048, 2048])).then_inc(y_zero, 16)
        pool.dma_start(relb[0:BUCKETS, :], rel_bias).then_inc(bsel_in, 16)
        pool.dma_start(bsel_sb[:, :], bias_sel).then_inc(bsel_in, 16)
        pool.wait_ge(bvec_rdy, 1)
        pool.dma_start(bvec_d, bvec_sb[:, :]).then_inc(bvec_out, 16)
        pool.wait_ge(bvec_out, 16)
        for g in range(GROUPS):
            pool.dma_start(brep_d[g].rearrange("q (h j) -> q h j", j=JB[g]),
                           bass.AP(bvec_d.tensor, JOFF[g], [[0, P], [NJ, HPG], [1, JB[g]]])).then_inc(brep_in, 16)
        pool.wait_ge(brep_in, 16 * GROUPS)

        def load_bias(g):
            if g == 1:
                pool.wait_ge(s_sb, HPG)
            if g == 2:
                pool.wait_ge(s_sb, 2 * HPG)
            n = JB[g] - P
            src = bass.AP(brep_d[g].tensor, P - 1, [[HPG * JB[g] - 1, P], [JB[g], HPG], [1, n]])
            pool.dma_start(bias[:, :, 0:n], src).then_inc(bias_in, 16)

        load_bias(0)
        load_bias(1)
        load_bias(2)
        pool.wait_ge(og_rdy, 2 * HPG)
        pool.dma_start(att_d[0].rearrange("(l r) c -> l r c", r=4),
                       Og[1][:, :, :, :].rearrange("p t h e -> p t (h e)")).then_inc(att_st[0], 16)
        pool.wait_ge(pv_ps, 2 * HPG)
        link(pool.memset(bpad[0][:, :], 0.0))
        link(pool.memset(bpad[1][:, :], 0.0))
        pool.sem_inc(zero_rdy, 1)
        pool.wait_ge(og_rdy, 3 * HPG)
        pool.dma_start(att_d[1].rearrange("(l r) c -> l r c", r=4),
                       Og[1][:, :, :, :].rearrange("p t h e -> p t (h e)")).then_inc(att_st[1], 16)
        for g in range(2):
            pool.wait_ge(att_st[g], 16)
            pool.dma_start((O1, O2)[g][:, :, :, :].rearrange("p t h e -> p t (h e)"),
                           att_d[g].rearrange("(t p) c -> p t c", p=P)).then_inc(att_ld, 16)
        pool.dma_start(x1[:, :, :], x.rearrange("(t p) d -> p t d", p=P)).then_inc(x1_in, 16)
        pool.wait_ge(yatt_rdy, 1)
        pool.wait_ge(out_rdy, [i for i, o in enumerate(outs) if o[0] == "yattT"][-1] + 1)
        pool.dma_start(ln_g[:, :], ln1_g.broadcast_to([P, D])).then_inc(ln_in, 16)
        pool.dma_start(ln_b[:, :], ln1_b.broadcast_to([P, D])).then_inc(ln_in, 16)
        pool.wait_ge(out_rdy, [i for i, o in enumerate(outs) if o[0] == "pa"][-1] + 1)
        pool.dma_start(wr_sb[:, :, :], w_router.rearrange("(k p) n -> p k n", p=P)).then_inc(ln_in, 16)
        for t in range(NT):
            pool.wait_ge(u2_rdy, t + 1)
            pool.dma_start(u2_d[P * t:P * t + P, :], u2[:, t, :]).then_inc(u2_st, 16)
        pool.wait_ge(slot_rdy, 1)
        pool.wait_ge(ids_zero, 16)
        for n in range(2 * NT):
            pool.indirect_dma_start(ids_d, bass.IndirectOffsetOnAxis(ap=slot_u[:, n:n + 1], axis=0),
                                    cst[:, TOKID + n % NT:TOKID + n % NT + 1], None).then_inc(ids_st, 16)
        pool.wait_ge(ids_st, 32 * NT)
        pool.dma_start(idsq[:, :], ids_d.rearrange("(i p) o -> i (p o)", p=P)).then_inc(ids_ld, 16)
        pool.wait_ge(u2_st, 16 * NT)
        pool.wait_ge(idx_rdy, 1)

        def gather(c, s, n):
            wait(pool, m_xt, c - 1)
            pool.tensor_copy(idxc[s], idx_u[:, bass.ds(c, 1)]).then_inc(idxc_rdy, 1)
            pool.wait_ge(idxc_rdy, c + 1)
            pool.sem_inc(idxc_seen, 1)
            pool.indirect_dma_start(xg[s][:, :], None, u2_d,
                                    bass.IndirectOffsetOnAxis(ap=idxc[s], axis=0)).then_inc(xg_in[s], 16)

        gather(0, 0, 0)
        gather(1, 1, 1)
        gather(2, 0, 2)
        with pool.Fori(1, pair_count(pool)) as i:
            gather(2 * i + 1, 1, None)
            gather(2 * i + 2, 0, None)
        npair = pair_count(pool)
        for s in range(2):
            pool.wait_ge(y_st[s], npair * 16)
            pool.sem_inc(idxc_seen, 1)
        for t in range(NT):
            if t >= 2:
                pool.wait_ge(fin_use, t - 1)
            for k, dst in ((0, ya), (1, yc)):
                pool.indirect_dma_start(dst[t % 2][:, :], None, y_d,
                                        bass.IndirectOffsetOnAxis(ap=slot_u[:, k * NT + t:k * NT + t + 1], axis=0)
                                        ).then_inc(fin_in[t % 2], 16)

    @block.tensor
    def _(pe):
        def tile_product(dst, lhs, rhs, n, done=None):
            for k in range(n):
                last = pe.matmul(dst, lhs(k), rhs(k), start=(k == 0), stop=(k == n - 1))
            if done is not None:
                last.then_inc(done, 1)
            return last

        pe.wait_ge(relb_one, 1)
        pe.wait_ge(bsel_in, 32)
        for g in range(GROUPS):
            dst = bank(2)[0:HPG, 0:JB[0]] if g == 0 else bank(3)[0:HPG, JOFF[g] - JOFF[1]:JOFF[g] - JOFF[1] + JB[g]]
            last = pe.matmul(dst, relb[:, HPG * g:HPG * g + HPG], bsel_sb[:, JOFF[g]:JOFF[g] + JB[g]],
                             start=True, stop=True)
        last.then_inc(bias_ps, 1)
        pe.wait_ge(small_in, 80)

        def out_step(i):
            kind, q, n = outs[i]
            dst = bank(i % 2)
            freed_wait(pe, i)
            if n is not None:
                pe.wait_ge(ring_in[n % 2], 16 * (n // 2 + 1))
            w = ring[n % 2] if n is not None else None
            qc = slice(P * q, P * q + P)
            if kind == "uT":
                pe.wait_ge(u_rdy, NT)
                for t in range(NT):
                    last = pe.transpose(dst[:, P * t:P * t + P], u_nat[:, t, P * q:P * q + P], ident)
            elif kind == "yT":
                pe.wait_ge(y_rdy, GH)
                for t in range(NT):
                    last = pe.transpose(dst[:, P * t:P * t + P], va[:, t, P * q:P * q + P], ident)
            elif kind == "yattT":
                pe.wait_ge(yatt_rdy, 1)
                yv = yatt[:, :, :, :].rearrange("p t h e -> p t (h e)")
                for t in range(NT):
                    last = pe.transpose(dst[:, P * t:P * t + P], yv[:, t, P * q:P * q + P], ident)
            elif kind == "lra":
                pe.wait_ge(lraw_in, 16)
                pe.wait_ge(out_act, KD)
                last = tile_product(dst[0:LOWRANK, :], lambda k: lra_w[:, k, :], lambda k: uT[:, k, :], KD)
            elif kind == "gp":
                pe.wait_ge(out_act, freed([j for j, o in enumerate(outs) if o[0] == "lra"][0])[1])
                last = pe.matmul(dst, wgg[:, qc], lraT[:, :], start=True, stop=True)
            elif kind in ("qa", "ka", "qd", "kd", "ga", "gd"):
                last = tile_product(dst, lambda k: w[:, k, qc], lambda k: uT[:, k, :], KD)
            elif kind in ("va", "ra"):
                last = tile_product(dst, lambda k: uT[:, k, qc], lambda k: w[:, k, :], KD)
            elif kind == "vd":
                g = group_of(n)
                last = tile_product(dst, lambda k: token_tile(k, g, q), lambda k: w[:, k, :], KD)
            elif kind == "pg":
                if q == 0:
                    pe.wait_ge(out_act, freed(max(j for j, o in enumerate(outs) if o[0] == "yT"))[1])
                qq = slice(P * (q % 4), P * (q % 4) + P)
                last = tile_product(dst, lambda k: w[:, k, qq], lambda k: yglaT[:, k, :], KD)
            elif kind == "pa":
                if q == 0:
                    pe.wait_ge(out_act, freed(max(j for j, o in enumerate(outs) if o[0] == "yattT"))[1])
                wv = w[:, :, :].rearrange("p (k a) n -> p k (a n)", a=2)
                last = tile_product(dst, lambda k: wv[:, k, qc], lambda k: yattT[:, k, :], 4)
            else:
                t = q // 2
                if q == 0:
                    pe.wait_ge(out_dve, freed(max(j for j, o in enumerate(outs) if o[0] == "pa"))[1])
                last = tile_product(dst, lambda k: mT[:, k, P * t:P * t + P], lambda k: w[:, k, :], KD)
            last.then_inc(out_rdy, 1)
        for kind, a in steps:
            if kind == "ada":
                pe.wait_ge(ada_sum, a + 1)
                if a >= 2:
                    pe.wait_ge(ada_out, a - 1)
                if a == 4:
                    pe.wait_ge(y_rdy, GH)
                if a >= 1:
                    pe.wait_ge(ada_out, a)
                pe.matmul(bank(7), ones, acc[a % 2][:, :], start=True, stop=True).then_inc(ada_ps, 1)
            elif kind == "z":
                out_step(a)
            elif kind == "gla_kt":
                pe.wait_ge(gla_fac, a + 1)
                if a:
                    pe.wait_ge(y_rdy, a)
                for t in range(NT):
                    last = pe.transpose(bank(6)[:, P * t:P * t + P], t2[:, P * t:P * t + P], ident)
                last.then_inc(kt_ps, 1)
            elif kind == "gla_kv":
                if a == 0:
                    pe.wait_ge(bvec_rdy, 1)
                    pe.wait_ge(out_act, freed(max(j for j, o in enumerate(outs) if o[0] == "va"))[1])
                for c in range(NCH):
                    p0 = CHUNK * (c % 2)
                    for i in range(NSUB):
                        q0 = CHUNK * c + SUB * i
                        last = pe.matmul(bank(7)[p0:p0 + CHUNK, CHUNK * (c // 2) + SUB * i:CHUNK * (c // 2) + SUB * i + SUB],
                                         KI[:, c, i, :], t1[:, q0:q0 + SUB], start=True, stop=True)
                last.then_inc(at_ps, 1)
                pe.wait_ge(kt_sb, a + 1)
                if a:
                    pe.wait_ge(st_sb, a)
                for c in range(NCH - 1):
                    p0 = CHUNK * (c % 2)
                    last = pe.matmul(kv_bank(c), kdN[p0:p0 + CHUNK, c // 2, :],
                                     va[p0:p0 + CHUNK, c // 2, GDV * a:GDV * a + GDV], start=True, stop=True)
                last.then_inc(kv_ps, 1)
            elif kind == "gla_o":
                pe.wait_ge(st_sb, a + 1)
                pe.wait_ge(at_sb, a + 1)
                for c in range(NCH):
                    p0 = CHUNK * (c % 2)
                    dst = ps[p0:p0 + CHUNK, 6 + c // 4, GDV * (c // 2 % 2):GDV * (c // 2 % 2) + GDV]
                    last = pe.matmul(dst, attT[p0:p0 + CHUNK, c // 2, :],
                                     va[p0:p0 + CHUNK, c // 2, GDV * a:GDV * a + GDV], start=True, stop=(c == 0))
                    if c:
                        last = pe.matmul(dst, t3[:, CHUNK * c:CHUNK * c + CHUNK], St[:, c, :], start=False, stop=True)
                last.then_inc(o_ps, 1)
            elif kind == "S":
                g, j = a // HPG, a % HPG
                if a == 0:
                    pe.wait_ge(st_sb, GH)
                if a:
                    pe.wait_ge(s_sb, a)
                if j == 0:
                    last_v = max(i for i, o in enumerate(outs) if o[0] == "vd" and group_of(o[2]) == g)
                    pe.wait_ge(out_act, freed(last_v)[1])
                f, p0 = j // 2, DH * (j % 2)
                q, k = qg[g % 2], kg[g % 2]
                for t in range(NT):
                    lhs = q[p0:p0 + DH, f, P * t:P * t + P]
                    if g == 0:
                        k0 = 0 if t else 1
                        dst = ps[:, 2 + t // 2, 256 * (t % 2) + P * k0:256 * (t % 2) + 256]
                        rhs = k[p0:p0 + DH, f, P * (t - 1 + k0):P * t + P]
                    else:
                        dst = ps[:, 2, P * t:P * t + P]
                        rhs = k[p0:p0 + DH, f, P * t:P * t + P]
                    last = pe.matmul(dst, lhs, rhs, start=True, stop=True)
                last.then_inc(s_ps, 1)
            elif kind == "T":
                g = a // HPG
                pe.wait_ge(p_sb, a + 1)
                if a:
                    pe.wait_ge(pt_sb, a)
                for t in range(NT):
                    for half in ((0, 1) if g == 0 else (0,)):
                        if g == 0 and t == 0 and half == 0:
                            continue
                        m = 2 * t + half if g == 0 else t
                        last = pe.transpose(ps[:, 4 + m // 4, P * (m % 4):P * (m % 4) + P],
                                            Pr[a % 2][:, t, P * half:P * half + P] if g == 0 else
                                            Pr[a % 2][:, t, 0:P], ident)
                last.then_inc(pt_ps, 1)
            elif kind == "PV":
                g, j = a // HPG, a % HPG
                pe.wait_ge(pt_sb, a + 1)
                if a:
                    pe.wait_ge(og_rdy, a)
                else:
                    pe.wait_ge(y_rdy, GH)
                v = vg[g % 2]
                for t in range(NT):
                    dst = bank(6)[:, DH * t:DH * t + DH]
                    if g == 0 and t:
                        pe.matmul(dst, PT[a % 2][:, 2 * t, :], v[:, t - 1, DH * j:DH * j + DH], start=True, stop=False)
                    m = 2 * t + 1 if g == 0 else t
                    last = pe.matmul(dst, PT[a % 2][:, m, :], v[:, t, DH * j:DH * j + DH],
                                     start=not (g == 0 and t), stop=True)
                last.then_inc(pv_ps, 1)

        for k in range(KD):
            pe.wait_ge(u2_rdy, NT)
            if k >= 2:
                pe.wait_ge(u2T_sb, k - 1)
            for t in range(NT):
                last = pe.transpose(bank(2 + k % 2)[:, P * t:P * t + P], u2[:, t, P * k:P * k + P], ident)
            last.then_inc(u2T_ps, 1)
        pe.wait_ge(u2T_sb, KD)
        pe.wait_ge(ln_in, 48)
        for t in range(NT):
            last = tile_product(bank(4)[:, 64 * t:64 * t + EG + NE], lambda k: u2T[:, k, P * t:P * t + P],
                                lambda k: wr_sb[:, k, :], KD)
        last.then_inc(lg_ps, 1)
        pe.wait_ge(rt_asg, 1)
        for t in range(NT):
            for tt in range(t + 1):
                pe.matmul(bank(5)[:, NE * t:NE * t + NE], cst[:, TRI:TRI + P] if tt == t else ones,
                          rt[:, 0, tt, :], start=(tt == 0), stop=(tt == t))
        for tt in range(NT):
            last = pe.matmul(bank(5)[:, NE * NT:NE * NT + NE], ones, rt[:, 0, tt, :], start=(tt == 0), stop=(tt == NT - 1))
        last.then_inc(rk_ps, 1)
        pe.wait_ge(ids_ld, 16)
        pe.transpose(bank(6)[:, 0:NCHUNK], idsq[:, :], cst[0:NCHUNK, IDENT:IDENT + NCHUNK]).then_inc(ids_ps, 1)

        def x_transposes(c, s, loads):
            pe.wait_ge(xg_in[s], 16 * loads)
            wait(pe, m_xT, 2 * c)
            for k in range(KD):
                last = pe.transpose(ps[:, 2 + k // 4, P * (k % 4):P * (k % 4) + P], xg[s][:, P * k:P * k + P], ident)
            last.then_inc(m_xt, 1)

        def chunk(i, s):
            c = 2 * i + s
            pe.wait_ge(wgi[s], 16 * (i + 1))
            pe.wait_ge(m_xT, 2 * c + 2)
            wait(pe, m_gs, c)
            tile_product(bank(0), lambda k: xT[s][:, k, :], lambda k: wg[s][:, k, :], KD, m_gate)
            pe.wait_ge(wui[s], 16 * (i + 1))
            wait(pe, m_h, c)
            tile_product(bank(1), lambda k: xT[s][:, k, :], lambda k: wu[s][:, k, :], KD, m_up)
            x_transposes(c + 1, 1 - s, i + 1 + s)
            pe.wait_ge(m_h, c + 1)
            for f in range(FF // P):
                last = pe.transpose(bank(4)[:, P * f:P * f + P], hb[:, P * f:P * f + P], ident)
            last.then_inc(m_hps, 1)
            pe.wait_ge(wdi[s], 16 * (i + 1))
            pe.wait_ge(m_hT, c + 1)
            wait(pe, m_ya, c)
            tile_product(bank(5), lambda k: hT[:, k, :], lambda k: wd[s][:, k, 0:512], FF // P, m_y0)
            wait(pe, m_yd, c)
            tile_product(bank(6), lambda k: hT[:, k, :], lambda k: wd[s][:, k, 512:1024], FF // P, m_y)

        pe.wait_ge(tab_rdy, 1)
        x_transposes(0, 0, 1)
        chunk(0, 0)
        chunk(0, 1)
        with pe.Fori(1, pair_count(pe)) as i:
            chunk(i, 0)
            chunk(i, 1)

    @block.scalar
    def _(act):
        def link(ins):
            own["act"] += 1
            ins.then_inc(act_own, 1)
            act.wait_ge(act_own, own["act"])

        act.wait_ge(small_in, 80)
        act.activation(csil, ccol, ACT.Sigmoid).then_inc(csil_act, 1)
        act.wait_ge(bias_ps, 1)
        act.copy(bvec_sb[:, 0:JB[0]], bank(2)[0:HPG, 0:JB[0]])
        link(act.copy(bvec_sb[:, JB[0]:NJ], bank(3)[0:HPG, 0:NJ - JB[0]]))
        act.sem_inc(bvec_rdy, 1)

        def evac(i):
            kind, q, n = outs[i]
            src = bank(i % 2)
            if kind in DVE_OUT and kind != "ra":
                return
            act.wait_ge(out_rdy, i + 1)
            if kind == "ra":
                m = sum(o[0] == "ra" for o in outs[:i])
                if m == 0:
                    act.wait_ge(bvec_out, 16)
                if m:
                    act.wait_ge(out_dve, freed([j for j, o in enumerate(outs) if o[0] == "ra"][m - 1])[1])
                act.activation(sig_t[:, :], src, ACT.Sigmoid).then_inc(sig_rdy, 1)
                return
            if kind == "uT":
                last = act.copy(uT[:, q, :], src)
            elif kind == "yT":
                last = act.copy(yglaT[:, q, :], src)
            elif kind == "yattT":
                last = act.copy(yattT[:, q, :], src)
            elif kind == "lra":
                last = act.copy(lraT[:, :], src[0:LOWRANK, :])
            elif kind == "qa":
                last = act.mul(qaT[:, q, :], src, GDK ** -0.5)
            elif kind == "ka":
                last = act.copy(kaT[:, q, :], src)
            elif kind == "va":
                c0 = items[n][2][1] - VA
                last = act.copy(va[:, q, c0:c0 + 512], src)
            elif kind in ("qd", "kd", "vd"):
                g = group_of(n)
                if kind == "qd" and q == 0 and g == 2:
                    act.wait_ge(pv_ps, HPG)
                if kind == "vd" and q == 0 and g == 0:
                    act.wait_ge(ids_zero, 16)
                if kind == "vd":
                    last = act.copy(vg[g % 2][:, q, :], src)
                else:
                    dst = (qg if kind == "qd" else kg)[g % 2][:, q, :]
                    last = act.copy(perm_out(dst, g), perm_in(src, g))
            else:
                c0 = (items[n][2][1] - (GA if kind == "ga" else GD)) // P
                last = act.activation((sga if kind == "ga" else sgd)[:, c0 + q, :], src, ACT.Sigmoid)
            last.then_inc(out_act, 1)

        for kind, a in steps:
            if kind == "z":
                evac(a)
            elif kind == "gla_args":
                act.wait_ge(gla_abs, a + 1)
                link(act.activation(t2[:, :], t2[:, :], ACT.Exp, scale=-1.0))
                act.activation(t2[:, :], t2[:, :], ACT.Ln, bias=1.0).then_inc(gla_ln, 1)
                act.wait_ge(gla_arg, a + 1)
                act.activation(t1[:, :], t1[:, :], ACT.Exp, scale=1.0 / TAU)
                act.activation(t2[:, :], t2[:, :], ACT.Exp, scale=1.0 / TAU)
                act.activation(t3[:, :], Bc[:, :], ACT.Exp, scale=1.0 / TAU)
                act.activation(Dl, Bc[:, :].rearrange("p (c s) -> p c s", s=CHUNK)[:, :, CHUNK - 1], ACT.Exp, scale=1.0 / TAU)
                ki = KI[:, :, :, :].rearrange("p c i s -> p (c i s)")
                act.activation(ki, ki, ACT.Exp, scale=1.0 / TAU).then_inc(gla_exp, 1)
            elif kind == "gla_o":
                act.wait_ge(o_ps, a + 1)
                for t in range(NT):
                    link(act.activation(sq_junk[:, :], ps[:, 6 + t // 2, GDV * (t % 2):GDV * (t % 2) + GDV], ACT.Square,
                                        accum_out=ssq[:, t:t + 1]))
                act.sem_inc(ssq_rdy, 1)
            elif kind == "S":
                g, j = a // HPG, a % HPG
                act.wait_ge(s_sb, a + 1)
                if a >= 2:
                    act.wait_ge(pt_ps, a - 1)
                if j == 0 and g == 2:
                    act.wait_ge(att_st[0], 16)
                og = Og[0 if g == 0 else 1]
                for t in range(NT):
                    w0, w1 = (0 if g == 0 and t else P if g == 0 else 0), (256 if g == 0 else P)
                    last = act.activation(Pr[a % 2][:, t, w0:w1], Ssb[a % 2][:, t, w0:w1], ACT.Exp,
                                          bias=nmx[a % 2][:, t:t + 1], accum_out=og[:, t, j, DH + 1:DH + 2])
                last.then_inc(p_sb, 1)
            elif kind == "PV":
                g, j = a // HPG, a % HPG
                act.wait_ge(pv_ps, a + 1)
                og = Og[0 if g == 0 else 1]
                link(act.copy(og[:, :, j, 0:DH], bank(6)[:, 0:NT * DH].rearrange("p (t e) -> p t e", e=DH)))
                act.sem_inc(og_rdy, 1)
            elif kind == "combine":
                act.wait_ge(cm_m, 1)
                act.activation(cmb[:, 0:3, :], cmb[:, 0:3, :], ACT.Exp).then_inc(cm_e, 1)

        for k in range(KD):
            act.wait_ge(u2T_ps, k + 1)
            act.copy(u2T[:, k, :], bank(2 + k % 2)).then_inc(u2T_sb, 1)
        act.wait_ge(rt_ge, 1)
        act.activation(rt_w[:, 0:16], rt_w[:, 0:16], ACT.Exp).then_inc(rt_gexp, 1)
        act.wait_ge(rt_ge, 2)
        act.activation(rt_w[:, 32:36], rt_w[:, 32:36], ACT.Exp).then_inc(rt_gexp, 1)

        def x_evac(c, s):
            act.wait_ge(m_xt, c + 1)
            wait(act, m_up, c - 1)
            for half in range(2):
                act.copy(xT[s][:, 4 * half:4 * half + 4, :],
                         bank(2 + half).rearrange("p (k c) -> p k c", c=C)).then_inc(m_xT, 1)

        def chunk(i, s):
            c = 2 * i + s
            act.wait_ge(m_gate, c + 1)
            wait(act, m_gs, c)
            act.activation(sgb[:, :], bank(0), ACT.Sigmoid).then_inc(m_sig, 1)
            x_evac(c + 1, 1 - s)
            act.wait_ge(m_y0, c + 1)
            wait(act, y_st[s], 16 * i)
            act.copy(yb[s][:, 0:512], bank(5)).then_inc(m_ya, 1)
            act.wait_ge(m_ya, c + 1)
            act.wait_ge(m_yd, c + 1)
            rows = y_d[bass.ds(c * C, C), :]
            act.dma_start(rows, yb[s][:, :]).then_inc(y_st[s], 16)

        act.wait_ge(tab_rdy, 1)
        x_evac(0, 0)
        chunk(0, 0)
        chunk(0, 1)
        with act.Fori(1, pair_count(act)) as i:
            chunk(i, 0)
            chunk(i, 1)
        act.dma_start(ln2gb[:, 0, :], ln2_g.broadcast_to([P, D])).then_inc(ln2_in, 16)
        act.dma_start(ln2gb[:, 1, :], ln2_b.broadcast_to([P, D])).then_inc(ln2_in, 16)
        for t in range(NT):
            act.wait_ge(fin_rdy, t + 1)
            act.dma_start(out[P * t:P * t + P, :], r2[t % 2][:, :]).then_inc(out_st[t % 2], 16)
        for s in range(2):
            act.wait_ge(out_st[s], 16 * NT // 2)

    @block.vector
    def _(dve):
        def link(ins):
            own["dve"] += 1
            ins.then_inc(dve_own, 1)
            dve.wait_ge(dve_own, own["dve"])

        def bc(ap, axis, n):
            v = ap.unsqueeze(axis)
            shape = list(v.shape)
            shape[axis] = n
            return v.broadcast_to(shape)

        dve.wait_ge(csil_act, 1)
        link(dve.tensor_tensor(csil, csil, ccol, ALU.mult))

        def ada_sum_up(b):
            n = ada_item[b]
            dve.wait_ge(ring_in[n % 2], 16 * (n // 2 + 1))
            dve.wait_ge(bpad_in[b % 2], 16 * (b // 2 + 1))
            if b >= 2:
                dve.wait_ge(ada_ps, b - 1)
            a = acc[b % 2]
            for k in range(KD):
                ins = dve.scalar_tensor_tensor(out=a[:, :], in0=ring[n % 2][:, k, :], scalar=csil[:, k:k + 1],
                                               in1=(bpad[b % 2] if k == 0 else a)[:, :], op0=ALU.mult, op1=ALU.add)
                if k == 0:
                    ins.then_inc(bpad_use, 1)
                    dve.wait_ge(bpad_use, b + 1)
                elif k < KD - 1:
                    link(ins)
                else:
                    ins.then_inc(ada_sum, 1)
                    dve.wait_ge(ada_sum, b + 1)
            dve.sem_inc(ring_dve, 1)

        def ada_move(b):
            dve.wait_ge(ada_ps, b + 1)
            mod, half = b // 2, slice(512 * (b % 2), 512 * (b % 2) + 512)
            dst = mods_a[:, mod, half] if mod < 2 else mods[:, mod - 2, half]
            add = 1.0 if mod in (1, 4) else 0.0
            dve.tensor_scalar(dst, bank(7), add, None, ALU.add).then_inc(ada_out, 1)

        def evac(i):
            kind, q, n = outs[i]
            src = bank(i % 2)
            if kind not in DVE_OUT or kind == "gp":
                return
            dve.wait_ge(out_rdy, i + 1)
            if kind == "ra":
                m = sum(o[0] == "ra" for o in outs[:i])
                if m == 0:
                    dve.wait_ge(gn_in, 16)
                c0 = items[n][2][1] - RA
                dve.wait_ge(sig_rdy, m + 1)
                d = sr[:, q, c0:c0 + 512]
                link(dve.tensor_tensor(d, src, sig_t[:, :], ALU.mult))
                link(dve.tensor_tensor(d, d, gn_b[:, c0:c0 + 512], ALU.mult))
                dve.sem_inc(out_dve, 1)
            elif kind == "pg":
                if q == 0:
                    dve.wait_ge(out_act, freed(max(j for j, o in enumerate(outs) if o[0] == "gd"))[1])
                dve.tensor_tensor(mT[:, q, :], src, sga[:, q, :], ALU.mult).then_inc(out_dve, 1)
            elif kind == "pa":
                link(dve.tensor_tensor(sgd[:, q, :], src, sgd[:, q, :], ALU.mult))
                link(dve.tensor_tensor(mT[:, q, :], mT[:, q, :], sgd[:, q, :], ALU.add))
                dve.sem_inc(out_dve, 1)
            else:
                t, half = q // 2, q % 2
                hs = slice(512 * half, 512 * half + 512)
                if q == 0:
                    dve.wait_ge(x1_in, 16)
                    dve.wait_ge(ada_out, 12)
                    dve.wait_ge(ln_in, 48)
                link(dve.tensor_tensor(lnt[0][:, hs], src, mods[:, 0, hs], ALU.mult))
                link(dve.scalar_tensor_tensor(out=x1[:, t, hs], in0=x1[:, t, hs], scalar=ALPHA, in1=lnt[0][:, hs],
                                              op0=ALU.mult, op1=ALU.add))
                dve.sem_inc(out_dve, 1)
                if half:
                    norm_rows(x1[:, t, :], ln_g[:, :], ln_b[:, :])
                    link(dve.tensor_tensor(u2[:, t, :], x1[:, t, :], mods[:, 2, :], ALU.mult))
                    dve.tensor_tensor(u2[:, t, :], u2[:, t, :], mods[:, 1, :], ALU.add).then_inc(u2_rdy, 1)

        def rsqrt(r, v, t):
            link(dve.tensor_scalar(r.bitcast(u32), v.bitcast(u32), -0.5, float(0x5F3759DF), ALU.mult, ALU.add))
            for _ in range(4):
                link(dve.scalar_tensor_tensor(out=t, in0=r, scalar=-0.5, in1=r, op0=ALU.mult, op1=ALU.mult))
                link(dve.tensor_tensor(t, t, v, ALU.mult))
                link(dve.scalar_tensor_tensor(out=r, in0=t, scalar=1.5, in1=r, op0=ALU.add, op1=ALU.mult))

        def norm_rows(v, g, b):
            dve.bn_stats(bnst[:, 0:6], v[:, 0:512])
            link(dve.bn_stats(bnst[:, 6:12], v[:, 512:1024]))
            link(dve.bn_aggr(bnag, bnst))
            link(dve.tensor_scalar(bnag[:, 1:2], bnag[:, 1:2], EPS, None, ALU.add))
            rsqrt(lrs, bnag[:, 1:2], rs_t[:, 0:1])
            link(dve.tensor_scalar(v, v, bnag[:, 0:1], lrs, ALU.subtract, ALU.mult))
            link(dve.tensor_tensor(v, v, g, ALU.mult))
            link(dve.tensor_tensor(v, v, b, ALU.add))

        for b in range(4):
            ada_sum_up(b)
            if b:
                ada_move(b - 1)
        ada_move(3)
        dve.wait_ge(ada_out, 4)
        dve.wait_ge(x_load, 16)
        for t in range(NT):
            link(dve.tensor_tensor(u_nat[:, t, :], x_in[:, t, :], mods_a[:, 1, :], ALU.mult))
            dve.tensor_tensor(u_nat[:, t, :], u_nat[:, t, :], mods_a[:, 0, :], ALU.add).then_inc(u_rdy, 1)

        Bb = Bc[:, :].rearrange("p (m s) -> p m s", s=SUB)
        Bch = Bc[:, :].rearrange("p (c s) -> p c s", s=CHUNK)
        Bref = Bc[:, :].rearrange("p (c i s) -> p c i s", c=NCH, i=NSUB)[:, :, :, SUB // 2 - 1]
        for kind, a in steps[4:]:
            if kind == "z":
                evac(a)
            elif kind == "gla_args":
                gp = [i for i, o in enumerate(outs) if o[0] == "gp" and o[1] == a][0]
                dve.wait_ge(out_rdy, gp + 1)
                if a == 0:
                    dve.wait_ge(bvec_out, 16)
                    dve.wait_ge(y_zero, 16)
                    dve.wait_ge(out_act, freed(max(j for j, o in enumerate(outs) if o[0] == "ka"))[1])
                if a:
                    dve.wait_ge(o_ps, a)
                link(dve.tensor_scalar(t1[:, :], bank(gp % 2), bgl[:, a:a + 1], None, ALU.add))
                dve.sem_inc(out_dve, 1)
                dve.scalar_tensor_tensor(out=t2[:, :], in0=t1[:, :], scalar=-1.0, in1=t1[:, :],
                                         op0=ALU.mult, op1=ALU.max).then_inc(gla_abs, 1)
                dve.wait_ge(gla_ln, a + 1)
                link(dve.scalar_tensor_tensor(out=t1[:, :], in0=t1[:, :], scalar=0.0, in1=t2[:, :],
                                              op0=ALU.min, op1=ALU.subtract))
                link(dve.tensor_tensor_scan(Bc[:, :], cst[:, RESET:RESET + S], t1[:, :], 0.0, ALU.mult, ALU.add))
                dve.tensor_tensor(KI[:, :, :, :], bc(Bref, 3, CHUNK), bc(Bch, 2, NSUB), ALU.subtract)
                dve.tensor_tensor(t1[:, :].rearrange("p (m s) -> p m s", s=SUB), Bb,
                                  bc(Bb[:, :, SUB // 2 - 1], 2, SUB), ALU.subtract)
                link(dve.tensor_tensor(t2[:, :].rearrange("p (c s) -> p c s", s=CHUNK), bc(Bch[:, :, CHUNK - 1], 2, CHUNK),
                                       Bch, ALU.subtract))
                ki = KI[:, :, :, :].rearrange("p c i s -> p (c i s)")
                dve.tensor_scalar(ki, ki, CLAMP * TAU, None, ALU.min)
                dve.tensor_scalar(t1[:, :], t1[:, :], CLAMP * TAU, None, ALU.min).then_inc(gla_arg, 1)
                dve.wait_ge(gla_exp, a + 1)
                kc = kaT[:, a, :].rearrange("p (c s) -> p c s", s=CHUNK)
                dve.tensor_tensor(t1[:, :], t1[:, :], qaT[:, a, :], ALU.mult)
                dve.tensor_tensor(t2[:, :], t2[:, :], kaT[:, a, :], ALU.mult)
                dve.tensor_tensor(t3[:, :], t3[:, :], qaT[:, a, :], ALU.mult)
                dve.tensor_tensor(KI[:, :, :, :], KI[:, :, :, :], bc(kc, 2, NSUB), ALU.mult).then_inc(gla_fac, 1)
            elif kind == "gla_kt":
                dve.wait_ge(kt_ps, a + 1)
                dve.tensor_copy(kdN[:, :, :], bank(6).rearrange("p (t k) -> p t k", k=P)).then_inc(kt_sb, 1)
            elif kind == "gla_kv":
                dve.wait_ge(at_ps, a + 1)
                dve.tensor_tensor(attT[:, :, :], bank(7)[:, 0:NT * CHUNK].rearrange("p (t s) -> p t s", s=CHUNK),
                                  bc(cst[:, GMASK:GMASK + CHUNK], 1, NT), ALU.mult).then_inc(at_sb, 1)
                dve.wait_ge(kv_ps, a + 1)
                link(dve.tensor_copy(St[:, 1, :], kv_bank(0)))
                for c in range(1, NCH - 1):
                    ins = dve.scalar_tensor_tensor(out=St[:, c + 1, :], in0=St[:, c, :], scalar=Dl[:, c:c + 1],
                                                   in1=kv_bank(c),
                                                   op0=ALU.mult, op1=ALU.add)
                    if c < NCH - 2:
                        link(ins)
                ins.then_inc(st_sb, 1)
            elif kind == "gla_o":
                dve.wait_ge(ssq_rdy, a + 1)
                link(dve.tensor_scalar(ssq, ssq, 1.0 / GDV, EPS, ALU.mult, ALU.add))
                rsqrt(rstd, ssq, rs_t)
                for t in range(NT):
                    ins = dve.scalar_tensor_tensor(out=va[:, t, GDV * a:GDV * a + GDV],
                                                   in0=ps[:, 6 + t // 2, GDV * (t % 2):GDV * (t % 2) + GDV],
                                                   scalar=rstd[:, t:t + 1], in1=sr[:, t, GDV * a:GDV * a + GDV],
                                                   op0=ALU.mult, op1=ALU.mult)
                ins.then_inc(y_rdy, 1)
            elif kind == "S":
                g, j = a // HPG, a % HPG
                dve.wait_ge(s_ps, a + 1)
                if j == 0:
                    dve.wait_ge(bias_in, (16, 32, 48)[g])
                if j == 0 and g == 2:
                    dve.wait_ge(att_st[0], 16)
                if a >= 2:
                    dve.wait_ge(p_sb, a - 1)
                ssb, og = Ssb[a % 2], Og[0 if g == 0 else 1]
                if g == 0:
                    pv = ps[:, 2:4, :].rearrange("p b (t k) -> p (b t) k", k=256)
                    dve.scalar_tensor_tensor(out=ssb[:, 1:4, :], in0=pv[:, 1:4, :], scalar=DH ** -0.5,
                                             in1=bc(bias[:, j, :], 1, 3), op0=ALU.mult, op1=ALU.add)
                    link(dve.scalar_tensor_tensor(out=ssb[:, 0, P:256], in0=pv[:, 0, P:256], scalar=DH ** -0.5,
                                                  in1=bias[:, j, P:256], op0=ALU.mult, op1=ALU.add))
                    dve.tensor_reduce(og[:, 1:4, j, DH:DH + 1], ssb[:, 1:4, :], AX.X, ALU.max)
                    link(dve.tensor_reduce(og[:, 0, j, DH:DH + 1], ssb[:, 0, P:256], AX.X, ALU.max))
                else:
                    link(dve.scalar_tensor_tensor(out=ssb[:, :, 0:P], in0=bank(2).rearrange("p (t k) -> p t k", k=P),
                                                  scalar=DH ** -0.5, in1=bc(bias[:, j, 0:P], 1, NT),
                                                  op0=ALU.mult, op1=ALU.add))
                    link(dve.tensor_reduce(og[:, :, j, DH:DH + 1], ssb[:, :, 0:P], AX.X, ALU.max))
                dve.tensor_scalar(nmx[a % 2], og[:, :, j, DH], -1.0, None, ALU.mult).then_inc(s_sb, 1)
            elif kind == "T":
                g = a // HPG
                dve.wait_ge(pt_ps, a + 1)
                if a >= 2:
                    dve.wait_ge(pv_ps, a - 1)
                if g == 0:
                    pv = ps[:, 4:6, :].rearrange("p b (m k) -> p (b m) k", k=P)
                    dve.tensor_copy(PT[a % 2][:, 1:8, :], pv[:, 1:8, :]).then_inc(pt_sb, 1)
                else:
                    dve.tensor_copy(PT[a % 2][:, 0:4, :], bank(4).rearrange("p (m k) -> p m k", k=P)).then_inc(pt_sb, 1)
            elif kind == "ada":
                if a == 4:
                    dve.wait_ge(zero_rdy, 2)
                ada_sum_up(a)
                ada_move(a)
            elif kind == "combine":
                dve.wait_ge(att_ld, 32)
                dve.wait_ge(og_rdy, 3 * HPG)
                O = [Og[0], O1, O2]
                f = [o[:, :, :, :].rearrange("p t h e -> p (t h) e") for o in O]
                link(dve.tensor_tensor(cmb[:, 3, :], f[0][:, :, DH], f[1][:, :, DH], ALU.max))
                link(dve.tensor_tensor(cmb[:, 3, :], cmb[:, 3, :], f[2][:, :, DH], ALU.max))
                for g in range(3):
                    ins = dve.tensor_tensor(cmb[:, g, :], f[g][:, :, DH], cmb[:, 3, :], ALU.subtract)
                ins.then_inc(cm_m, 1)
                dve.wait_ge(cm_e, 1)
                for g in range(3):
                    link(dve.tensor_tensor(cmb[:, 4 + g, :], cmb[:, g, :], f[g][:, :, DH + 1], ALU.mult))
                link(dve.tensor_tensor(cmb[:, 4, :], cmb[:, 4, :], cmb[:, 5, :], ALU.add))
                link(dve.tensor_tensor(cmb[:, 4, :], cmb[:, 4, :], cmb[:, 6, :], ALU.add))
                link(dve.reciprocal(cmb[:, 4, :], cmb[:, 4, :]))
                for g in range(3):
                    link(dve.tensor_tensor(cmb[:, g, :], cmb[:, g, :], cmb[:, 4, :], ALU.mult))
                yv = yatt[:, :, :, :].rearrange("p t h e -> p (t h) e")
                link(dve.tensor_tensor(yv, f[0][:, :, 0:DH], bc(cmb[:, 0, :], 2, DH), ALU.mult))
                for g in (1, 2):
                    link(dve.tensor_tensor(f[g][:, :, 0:DH], f[g][:, :, 0:DH], bc(cmb[:, g, :], 2, DH), ALU.mult))
                    link(dve.tensor_tensor(yv, yv, f[g][:, :, 0:DH], ALU.add))
                dve.sem_inc(yatt_rdy, 1)

        dve.wait_ge(lg_ps, 1)
        lgv = bank(4)[:, 0:64 * NT].rearrange("p (t n) -> p t n", n=64)
        gl = rt_w[:, 0:16].rearrange("p (t g) -> p t g", g=EG)
        el, elm = rt[:, 1, :, :], rt[:, 2, :, :]
        tmp, A = rt[:, 3, :, :], rt[:, 0, :, :]
        red = rt_w[:, 16:20]
        oh_g = rt_w[:, 48:64].rearrange("p (t g) -> p t g", g=EG)
        gsum, v1, v2, w1, w2 = (rt_w[:, n:n + 4] for n in (20, 24, 28, 36, 40))

        def first_max(v, onehot, vmax, rank, n, scratch):
            link(dve.tensor_reduce(vmax, v, AX.X, ALU.max))
            link(dve.tensor_tensor(scratch, v, bc(vmax, 2, n), ALU.is_equal))
            link(dve.tensor_tensor(scratch, scratch, bc(rank, 1, NT), ALU.mult))
            link(dve.tensor_reduce(red, scratch, AX.X, ALU.max))
            link(dve.tensor_tensor(onehot, scratch, bc(red, 2, n), ALU.is_equal))

        link(dve.tensor_tensor(gl, lgv[:, :, 0:EG], bc(brt[:, 0:EG], 1, NT), ALU.add))
        link(dve.tensor_tensor(el, lgv[:, :, EG:EG + NE], bc(brt[:, EG:EG + NE], 1, NT), ALU.add))
        g4 = rt[:, 4, 0, 0:16].rearrange("p (t g) -> p t g", g=EG)
        first_max(gl, oh_g, v1, cst[:, FIRST4:FIRST4 + EG], EG, g4)
        dve.tensor_tensor(gl, gl, bc(v1, 2, EG), ALU.subtract).then_inc(rt_ge, 1)
        link(dve.tensor_scalar(oh_g, oh_g, 1.0, -MASKED, ALU.subtract, ALU.mult))
        link(dve.tensor_tensor(elm.rearrange("p t (g e) -> p t g e", g=EG), el.rearrange("p t (g e) -> p t g e", g=EG),
                               bc(oh_g, 3, EPG), ALU.add))
        m1, m2 = rt_mask[:, 0, :, :], rt_mask[:, 1, :, :]
        dve.wait_ge(rt_gexp, 1)
        link(dve.tensor_reduce(gsum, gl, AX.X, ALU.add))
        first_max(elm, m1, v1, cst[:, FIRST32:FIRST32 + NE], NE, tmp)
        link(dve.scalar_tensor_tensor(out=elm, in0=m1, scalar=3.0 * MASKED, in1=elm, op0=ALU.mult, op1=ALU.add))
        first_max(elm, m2, v2, cst[:, FIRST32:FIRST32 + NE], NE, tmp)
        dve.tensor_tensor(A, m1, m2, ALU.add).then_inc(rt_asg, 1)
        dve.tensor_tensor(rt_w[:, 32:36], v2, v1, ALU.subtract).then_inc(rt_ge, 1)
        dve.wait_ge(rt_gexp, 2)
        ex = rt_w[:, 32:36]
        link(dve.tensor_scalar(w1, ex, 1.0, None, ALU.add))
        link(dve.tensor_tensor(w1, w1, gsum, ALU.mult))
        link(dve.reciprocal(w1, w1))
        link(dve.tensor_tensor(w2, w1, ex, ALU.mult))
        dve.tensor_copy(slot_w[:, 0:4], w1)
        dve.tensor_copy(slot_w[:, 4:8], w2)
        dve.wait_ge(rk_ps, 1)
        cnt, xe, inc, xb, tm = (rt[:, n, 0, :] for n in (4, 5, 6, 7, 8))
        link(dve.tensor_copy(cnt, bank(5)[:, NE * NT:NE * NT + NE]))
        link(dve.tensor_scalar(xe, cnt, float(C), None, ALU.is_gt))
        for m in (2, 3):
            link(dve.tensor_scalar(tm, cnt, float(m * C), None, ALU.is_gt))
            link(dve.tensor_tensor(xe, xe, tm, ALU.add))
        link(dve.tensor_tensor_scan(inc, ones[:, 0:NE], xe, 0.0, ALU.mult, ALU.add))
        link(dve.tensor_tensor(xb, inc, xe, ALU.subtract))
        link(dve.tensor_scalar(xb, xb, float(NE - 1), float(C), ALU.add, ALU.mult))
        link(dve.tensor_tensor(xb, xb, cst[:, E128:E128 + NE], ALU.subtract))
        rk = bank(5)[:, 0:NE * NT].rearrange("p (t n) -> p t n", n=NE)
        link(dve.tensor_scalar(tmp, rk, float(C), None, ALU.is_ge))
        link(dve.tensor_tensor(tmp, tmp, bc(xb, 1, NT), ALU.mult))
        link(dve.tensor_tensor(tmp, tmp, bc(cst[:, E128:E128 + NE], 1, NT), ALU.add))
        link(dve.tensor_tensor(tmp, tmp, rk, ALU.add))
        for k, m in enumerate((m1, m2)):
            link(dve.tensor_tensor(el, tmp, m, ALU.mult))
            link(dve.tensor_reduce(rt_w[:, 48 + 4 * k:52 + 4 * k], el, AX.X, ALU.add))
        link(dve.tensor_copy(slot_u, rt_w[:, 48:56]))
        dve.sem_inc(slot_rdy, 1)
        link(dve.tensor_copy(ctab_f[:, 0:NE], cst[:, I32:I32 + NE]))
        le = rt[:, 2:4, :, :].rearrange("p a t n -> p (a t) n")
        link(dve.tensor_tensor(le, bc(inc, 1, 8), bc(cst[:, J8:J8 + 8], 2, NE), ALU.is_le))
        link(dve.tensor_reduce(ctab_f[:, NE:NE + 8], le, AX.X, ALU.add))
        link(dve.tensor_scalar(ctab_f[:, NE:NE + 8], ctab_f[:, NE:NE + 8], float(NE - 1), None, ALU.min))
        link(dve.tensor_scalar(tm[:, 0:4], cst[:, EVEN:EVEN + 4], inc[:, NE - 1:NE], None, ALU.is_lt))
        link(dve.tensor_reduce(ctab_f[:, NCHUNK:NCHUNK + 1], tm[:, 0:4], AX.X, ALU.add))
        link(dve.tensor_scalar(ctab_f[:, NCHUNK:NCHUNK + 1], ctab_f[:, NCHUNK:NCHUNK + 1], float(NE // 2), None, ALU.add))
        link(dve.memset(ctab_f[:, NCHUNK - 1:NCHUNK], 0.0))
        link(dve.tensor_copy(tab_u[:, 0:NCHUNK + 1], ctab_f[:, 0:NCHUNK + 1]))
        dve.sem_inc(tab_rdy, 1)
        dve.wait_ge(ids_ps, 1)
        dve.tensor_copy(idx_u[:, 0:NCHUNK], bank(6)[:, 0:NCHUNK]).then_inc(idx_rdy, 1)

        def chunk(i, s):
            c = 2 * i + s
            dve.wait_ge(m_sig, c + 1)
            wait(dve, m_h, c)
            dve.tensor_tensor(gsb[:, :], bank(0), sgb[:, :], ALU.mult).then_inc(m_gs, 1)
            dve.wait_ge(m_up, c + 1)
            dve.wait_ge(m_gs, c + 1)
            wait(dve, m_hps, c)
            dve.tensor_tensor(hb[:, :], bank(1), gsb[:, :], ALU.mult).then_inc(m_h, 1)
            dve.wait_ge(m_hps, c + 1)
            wait(dve, m_y, c)
            dve.tensor_copy(hT[:, :, :], bank(4).rearrange("p (f c) -> p f c", c=C)).then_inc(m_hT, 1)
            dve.wait_ge(m_y, c + 1)
            wait(dve, y_st[s], 16 * i)
            dve.tensor_copy(yb[s][:, 512:1024], bank(6)).then_inc(m_yd, 1)

        dve.wait_ge(tab_rdy, 1)
        chunk(0, 0)
        chunk(0, 1)
        with dve.Fori(1, pair_count(dve)) as i:
            chunk(i, 0)
            chunk(i, 1)
        dve.wait_ge(ln2_in, 32)
        for t in range(NT):
            s = t % 2
            dve.wait_ge(fin_in[s], 32 * (t // 2 + 1))
            if t >= 2:
                dve.wait_ge(out_st[s], 16 * (t // 2))
            a, b, r = ya[s][:, :], yc[s][:, :], r2[s][:, :]
            link(dve.tensor_scalar(a, a, slot_w[:, t:t + 1], None, ALU.mult))
            link(dve.scalar_tensor_tensor(out=a, in0=b, scalar=slot_w[:, NT + t:NT + t + 1], in1=a, op0=ALU.mult, op1=ALU.add))
            link(dve.tensor_tensor(a, a, mods[:, 3, :], ALU.mult))
            link(dve.scalar_tensor_tensor(out=r, in0=x1[:, t, :], scalar=ALPHA, in1=a, op0=ALU.mult, op1=ALU.add))
            dve.sem_inc(fin_use, 1)
            norm_rows(r, ln2gb[:, 0, :], ln2gb[:, 1, :])
            dve.sem_inc(fin_rdy, 1)

    ctx.close()


def kernel(x, c, rel_bias, w_ada, b_ada, w_in, w_gla_gate, b_gla_gate, gla_norm, w_proj_gla, w_proj_attn,
           w_out, ln1_g, ln1_b, w_router_group, b_router_group, w_router_expert, b_router_expert,
           w_exp_gate, w_exp_up, w_exp_down, ln2_g, ln2_b):
    import concourse.bacc as bacc
    from concourse.bass_utils import run_bass_kernel_spmd

    def a(v):
        return np.ascontiguousarray(np.asarray(v))

    feeds = [
        a(x[0]), a(np.asarray(c).reshape(KD, P).T), a(rel_bias), a(w_ada[0]), a(b_ada), a(w_in[0]), a(w_gla_gate[0]),
        a(np.asarray(b_gla_gate).reshape(GH, GDK).T), a(gla_norm), a(w_proj_gla[0]), a(w_proj_attn[0]), a(w_out[0]),
        a(ln1_g), a(ln1_b),
        a(np.concatenate([np.asarray(w_router_group[0]), np.asarray(w_router_expert[0])], axis=1)),
        a(np.concatenate([np.asarray(b_router_group[0]), np.asarray(b_router_expert[0])])),
        a(w_exp_gate[0]).reshape(NE, D, FF), a(w_exp_up[0]).reshape(NE, D, FF), a(w_exp_down[0]).reshape(NE, FF, D),
        a(ln2_g), a(ln2_b), shape_constants(), bias_selectors(),
    ]
    nc = bacc.Bacc("TRN2", target_bir_lowering=False, num_devices=1)
    arrays, args = {}, []
    for n, v in enumerate(feeds):
        arrays[f"in{n}"] = v
        args.append(nc.dram_tensor(f"in{n}", v.shape, mybir.dt.from_np(v.dtype), kind="ExternalInput").ap())
    out = nc.dram_tensor("out", (S, D), mybir.dt.float32, kind="ExternalOutput").ap()
    build(nc, *args, out)
    r = run_bass_kernel_spmd(nc, [arrays], core_ids=[0])
    return r.results[0]["out"].reshape(1, S, D)
```

```python
import concourse.bass as bass
from concourse import mybir
from contextlib import ExitStack
import math
import numpy as np

P = 128
D = 1024
S = 512
KD = D // P
NT = S // P
N_MOD = 6
GH, GDK, GDV = 4, 128, 256
CHUNK, SUB = 64, 16
NCH, NSUB = S // CHUNK, CHUNK // SUB
LOWRANK, TAU = 16, 16.0
GROUPS, HPG, DH = 3, 8, 64
STEP = (1, 4, 4)
BUCKETS, MAX_DIST = 32, 2048
MASKED = -1.0e30
EPS = 1e-5
ALPHA = 2.0 ** 0.25
EG, EPG = 4, 8
NE = EG * EPG
FF = D // 2
C = 128
MAX_EXTRA = 8
NCHUNK = NE + MAX_EXTRA + 1
CLAMP = 40.0

QA, KA, VA, RA = 0, 512, 1024, 2048
LRA = 3072
QD = LRA + LOWRANK
KDL, VD = QD + 1536, QD + 3072
GA = VD + 1536
GD = GA + D

IDENT, ONES, TRI, GMASK, RESET, FIRST4, FIRST32, E128, J8, EVEN, TOKID, I32 = np.cumsum(
    [0, 128, 128, 128, 64, 512, 4, 32, 32, 8, 4, 4]).tolist()
NCONST = I32 + 32
JB = (384, 256, 256)
JOFF = (0, 384, 640)
NJ = 896


def shape_constants():
    c = np.zeros((P, NCONST), np.float32)
    p = np.arange(P)[:, None]
    c[:, IDENT:IDENT + P] = np.eye(P)
    c[:, ONES:ONES + P] = 1.0
    c[:, TRI:TRI + P] = p < np.arange(P)[None, :]
    c[:, GMASK:GMASK + CHUNK] = (p % CHUNK) <= np.arange(CHUNK)[None, :]
    c[:, RESET:RESET + S] = (np.arange(S) % CHUNK != 0)
    c[:, FIRST4:FIRST4 + 4] = 4 - np.arange(4)
    c[:, FIRST32:FIRST32 + 32] = 32 - np.arange(32)
    c[:, E128:E128 + 32] = C * np.arange(32)
    c[:, J8:J8 + 8] = np.arange(8)
    c[:, EVEN:EVEN + 4] = 2 * np.arange(4)
    c[:, TOKID:TOKID + 4] = p + P * np.arange(4)
    c[:, I32:I32 + 32] = np.arange(32)
    return c


def t5_bucket(dist):
    exact = BUCKETS // 2
    d = np.maximum(dist, 1).astype(np.float32)
    big = exact + (np.log(d / np.float32(exact)) / np.float32(math.log(MAX_DIST / exact))
                   * np.float32(BUCKETS - exact)).astype(np.int32)
    return np.where(dist < exact, dist, np.minimum(big, BUCKETS - 1))


def bias_selectors():
    sel = np.zeros((BUCKETS + 1, NJ), np.float32)
    for g, (first, last, unit, every) in enumerate(((255, 128, 1, 1), (127, 127, 4, 1), (127, 127, 4, 4))):
        for j in range(JB[g]):
            m = first - j
            if 0 <= m <= last and m % every == 0:
                sel[t5_bucket(np.array(m * unit)), JOFF[g] + j] = 1.0
            else:
                sel[BUCKETS, JOFF[g] + j] = MASKED
    return sel


def build(nc, x, c_col, rel_bias, w_ada, b_ada, w_in, w_gla_gate, b_gla, gla_norm, w_pg, w_pa, w_out,
          ln1_g, ln1_b, w_router, b_router, w_gate, w_up, w_down, ln2_g, ln2_b, const, bias_sel, out):
    f32, u32 = mybir.dt.float32, mybir.dt.uint32
    ALU, ACT, AX = mybir.AluOpType, mybir.ActivationFunctionType, mybir.AxisListType
    ctx = ExitStack()
    BASE = 16512

    def at(name, kb, shape, dt=f32):
        return nc.alloc_sbuf_tensor_at(name, shape, dt, offset=BASE + int(kb * 1024))

    def sem(name):
        return ctx.enter_context(nc.semaphore(name))

    def dram(name, shape, dt=f32):
        return nc.dram_tensor(name, shape, dt, kind="Internal").ap()

    uT = at("uT", 0, [P, KD, S])
    mT = at("mT", 0, [P, KD, S])
    ring = [at(f"ring{i}", 16 + 16 * i, [P, 8, 512]) for i in range(2)]
    qaT = at("qaT", 48, [P, GH, S])
    kaT = at("kaT", 56, [P, GH, S])
    yglaT = at("yglaT", 48, [P, KD, S])
    u2 = at("u2", 48, [P, NT, D])
    x_in = at("x_in", 64, [P, NT, D])
    va = at("va", 64, [P, NT, D])
    sga = at("sga", 64, [P, KD, S])
    u2T = at("u2T", 64, [P, KD, S])
    u_nat = at("u_nat", 80, [P, NT, D])
    sr = at("sr", 80, [P, NT, D])
    sgd = at("sgd", 80, [P, KD, S])
    qg = [at(f"qg{i}", 96 + 24 * i, [P, 4, S]) for i in range(2)]
    kg = [at(f"kg{i}", 104 + 24 * i, [P, 4, S]) for i in range(2)]
    vg = [at(f"vg{i}", 112 + 24 * i, [P, NT, 512]) for i in range(2)]
    x1 = at("x1", 96, [P, NT, D])
    mods = at("mods", 120, [P, 4, D])
    mods_a = at("mods_a", 120, [P, 2, D])
    acc = [at(f"acc{i}", 136 + 2 * i, [P, 512]) for i in range(2)]
    bpad = [at(f"bpad{i}", 140 + 2 * i, [P, 512]) for i in range(2)]
    t1 = at("t1", 144, [P, S])
    t2 = at("t2", 146, [P, S])
    t3 = at("t3", 148, [P, S])
    Bc = at("Bc", 150, [P, S])
    KI = at("KI", 152, [P, NCH, NSUB, CHUNK])
    St = at("St", 160, [P, NCH, GDV])
    gn_b = at("gn_b", 160, [P, D])
    kdN = at("kdN", 168, [P, NT, P])
    attT = at("attT", 170, [P, NT, CHUNK])
    sq_junk = at("sq_junk", 171, [P, GDV])
    sig_t = at("sig_t", 144, [P, 512])
    Ssb = [at(f"Ssb{i}", 144 + 12 * i, [P, 4, 256]) for i in range(2)]
    Pr = [at(f"Pr{i}", 148 + 12 * i, [P, 4, 256]) for i in range(2)]
    PT = [at(f"PT{i}", 152 + 12 * i, [P, 8, P]) for i in range(2)]
    OW = DH + 2
    Og = [at(f"Og{i}", 173 + 8.25 * i, [P, NT, HPG, OW]) for i in range(2)]
    bias = at("bias", 189.5, [P, HPG, 256])
    bvec_sb = at("bvec_sb", 144, [HPG, NJ])
    bsel_sb = at("bsel_sb", 148, [BUCKETS + 1, NJ])
    relb = at("relb", 151.75, [BUCKETS + 1, GROUPS * HPG])
    O1 = at("O1", 144, [P, NT, HPG, OW])
    O2 = at("O2", 152.25, [P, NT, HPG, OW])
    cmb = at("cmb", 160.5, [P, 8, 32])
    yatt = at("yatt", 161.5, [P, NT, HPG, DH])
    yattT = at("yattT", 189.5, [P, 4, S])
    ln_g = at("ln_g", 144, [P, D])
    ln_b = at("ln_b", 148, [P, D])
    lnt = [at(f"lnt{i}", 152 + 4 * i, [P, D]) for i in range(2)]
    r32 = mybir.dt.float32r
    wg = [at(f"wg{i}", 64 * i, [P, KD, FF]) for i in range(2)]
    wg_lo = [at(f"wg_lo{i}", 64 * i, [P, KD, FF], r32) for i in range(2)]
    wg_hi = [at(f"wg_hi{i}", 64 * i + 16, [P, KD, FF], r32) for i in range(2)]
    wu, wu_lo, wu_hi = at("wu", 32, [P, KD, FF]), at("wu_lo", 32, [P, KD, FF], r32), at("wu_hi", 48, [P, KD, FF], r32)
    FD = FF // P
    wd, wd_lo, wd_hi = at("wd", 96, [P, FD, D]), at("wd_lo", 96, [P, FD, D], r32), at("wd_hi", 136, [P, FD, D], r32)
    xg = [at(f"xg{i}", 152 + 4 * i, [P, D]) for i in range(2)]
    xT_hi, xT_lo = at("xT_hi", 160, [P, KD, C], r32), at("xT_lo", 164, [P, KD, C], r32)
    sgb = at("sgb", 168, [P, FF])
    gsb = at("gsb", 170, [P, FF])
    hb = at("hb", 172, [P, FF])
    hT_hi, hT_lo = at("hT_hi", 174, [P, FD, C], r32), at("hT_lo", 176, [P, FD, C], r32)
    yb = [at(f"yb{i}", 178 + 4 * i, [P, D]) for i in range(2)]
    ya = [at(f"ya{i}", 64 + 4 * i, [P, D]) for i in range(2)]
    yc = [at(f"yc{i}", 72 + 4 * i, [P, D]) for i in range(2)]
    r2 = [at(f"r2{i}", 80 + 4 * i, [P, D]) for i in range(2)]
    ln2gb = at("ln2gb", 88, [P, 2, D])
    cst = at("cst", 197.5, [P, NCONST])
    lraT = at("lraT", 202, [LOWRANK, S])
    wgg = at("wgg", 204, [LOWRANK, 512])
    rt_mask = at("rt_mask", 112, [P, 2, NT, NE])
    rt = at("rt", 113, [P, 10, NT, NE])
    rt_w = at("rt_w", 118, [P, 64])
    idsq = at("idsq", 118.5, [NCHUNK, P])
    lra_w = at("lra_w", 96, [P, KD, LOWRANK])
    wr_sb = at("wr_sb", 196.25, [P, KD, EG + NE])
    sm = at("sm", 206, [P, 192])
    csil, ccol = sm[:, 0:8], sm[:, 8:16]
    bgl = sm[:, 16:20]
    Dl = sm[:, 20:28]
    ssq, rstd = sm[:, 28:32], sm[:, 32:36]
    nmx = [sm[:, 36:40], sm[:, 40:44]]
    brt = sm[:, 44:80]
    bnst, bnag = sm[:, 80:92], sm[:, 92:94]
    lrs = sm[:, 94:95]
    ctab_f = sm[:, 96:96 + 48]
    slot_w = sm[:, 144:152]
    rs_t = sm[:, 152:156]
    ui = at("ui", 206.75, [P, 64], u32)
    slot_u = ui[:, 0:8]
    idx_u = ui[:, 8:8 + 48]
    idxc = [ui[:, 56:57], ui[:, 58:59]]
    tab_u = at("tab_u", 119.25, [P, 48], u32)

    ident = cst[:, IDENT:IDENT + P]
    ones = cst[:, ONES:ONES + P]

    ps = ctx.enter_context(nc.psum_tensor("ps", [P, 8, 512], f32))

    def bank(i):
        return ps[:, i, :]

    bvec_d = dram("bvec_d", [HPG, NJ])
    brep_d = [dram(f"brep_d{g}", [P, HPG * JB[g]]) for g in range(GROUPS)]
    att_d = [dram(f"att_d{g}", [S, HPG * OW]) for g in range(2)]
    u2_d = dram("u2_d", [S, D])
    x1_d = dram("x1_d", [S, D])
    ids_d = dram("ids_d", [NCHUNK * C, 1])
    y_d = dram("y_d", [(NCHUNK - 1) * C, D])

    def cols(w, c0, n=512):
        return w[:, c0:c0 + n].rearrange("(k p) n -> p k n", p=P)

    items = []

    def ada(b):
        items.append(("dve", cols(w_ada, 512 * b), ("ada", b)))

    def zblk(name, c0):
        items.append(("pe", cols(w_in, c0), (name, c0)))

    for b in range(4):
        ada(b)
    zblk("qa", QA), zblk("ka", KA)
    zblk("va", VA), zblk("va", VA + 512), zblk("ra", RA), zblk("ra", RA + 512)
    for g in range(GROUPS):
        zblk("qd", QD + 512 * g), zblk("kd", KDL + 512 * g), zblk("vd", VD + 512 * g)
    def wide(name, src, c0=0):
        items.append(("pe", src, (name, c0)))

    zblk("ga", GA), zblk("ga", GA + 512)
    ada(4), zblk("gd", GD)
    ada(5), zblk("gd", GD + 512)
    ada(6), wide("pg", cols(w_pg, 0), 0)
    ada(7), wide("pg", cols(w_pg, 512), 512)
    ada(8), wide("pa", w_pa.rearrange("(k p) n -> p k n", p=P))
    ada(9), wide("wo", cols(w_out, 0), 0)
    wide("wo", cols(w_out, 512), 512)
    ada(10), ada(11)
    slot, rank, before = {}, {}, {}
    first_gate = [n for n, it in enumerate(items) if it[2][0] == "ga"][0]
    tail = (0, 1, 0, 0, 1, 1, 0, 0, 1, 1, 0, 0, 1, 1, 0, 1, 0)
    for n in range(len(items)):
        slot[n] = n % 2 if n < first_gate else (first_gate + tail[n - first_gate]) % 2
        same = [m for m in range(n) if slot[m] == slot[n]]
        rank[n], before[n] = len(same), same[-1] if same else None
    dve_rank = {}
    for n, it in enumerate(items):
        if it[0] == "dve":
            dve_rank[n] = len(dve_rank)
    ada_item = {it[2][1]: n for n, it in enumerate(items) if it[2][0] == "ada"}

    outs = [("uT", k, None) for k in range(KD)]
    steps = [("ada", b) for b in range(4)] + [("z", n) for n in range(KD)]

    def z(o):
        outs.append(o)
        steps.append(("z", len(outs) - 1))

    def block_outs(n, kind):
        return [(kind, q, n) for q in range(4)]

    queue = []
    for n, it in enumerate(items):
        if it[0] == "pe" and it[2][0] in ("qa", "ka", "va", "ra", "qd", "kd", "vd", "ga", "gd"):
            queue.append(block_outs(n, it[2][0]))
    gla_q, att_q, gate_q = queue[:6], queue[6:15], queue[15:]
    z(("lra", 0, None))
    for o in sum(gla_q, []):
        z(o)
    g0 = sum(att_q[0:3], [])
    for h in range(GH):
        z(("gp", h, None))
        steps.append(("gla_args", h))
        z(g0[3 * h]), z(g0[3 * h + 1])
        steps.append(("gla_kt", h))
        steps.append(("gla_kv", h))
        z(g0[3 * h + 2])
        steps.append(("gla_o", h))
    for k in range(KD):
        z(("yT", k, None))
    for g in range(2):
        zs = sum(att_q[3 * g + 3:3 * g + 6], [])
        for j in range(HPG):
            a = g * HPG + j
            if a and j == 0:
                steps.append(("PV", a - 1))
            steps.append(("S", a))
            z(zs.pop(0))
            steps.append(("T", a))
            if j:
                steps.append(("PV", a - 1))
            if j % 2:
                z(zs.pop(0))
    zs = sum(gate_q, [])
    for j in range(HPG):
        a = 2 * HPG + j
        if j == 0:
            steps.append(("PV", a - 1))
            z(zs.pop(0))
        steps.append(("S", a))
        if j:
            z(zs.pop(0))
        steps.append(("T", a))
        if j:
            steps.append(("PV", a - 1))
        z(zs.pop(0))
        if j in (2, 4, 6):
            steps.append(("ada", 3 + j // 2))
    steps.append(("PV", 3 * HPG - 1))
    pgn = [n for n, it in enumerate(items) if it[2][0] == "pg"]
    pan = [n for n, it in enumerate(items) if it[2][0] == "pa"][0]
    won = [n for n, it in enumerate(items) if it[2][0] == "wo"]
    for ct in range(KD):
        z(("pg", ct, pgn[ct // 4]))
        if ct in (1, 6):
            steps.append(("ada", 7 if ct == 1 else 8))
    steps.append(("combine", 0))
    for t in range(4):
        z(("yattT", t, None))
    for ct in range(KD):
        z(("pa", ct, pan))
        if ct == 1:
            steps.append(("ada", 9))
    for t in range(NT):
        for half in range(2):
            z(("wo", 2 * t + half, won[half]))
    steps.append(("ada", 10)), steps.append(("ada", 11))
    LAST = {}
    for i, o in enumerate(outs):
        if o[2] is not None:
            LAST[o[2]] = i
    DVE_OUT = ("ra", "gp", "pg", "pa", "wo")

    def freed(i):
        e = outs[i][0] in DVE_OUT
        return e, sum((o[0] in DVE_OUT) == e for o in outs[:i + 1])

    ring_in = [sem(f"ring_in{i}") for i in range(2)]
    ring_dve = sem("ring_used_by_dve")
    small_in, x_load, gn_in, lraw_in, bpad_in = sem("small_in"), sem("x_load"), sem("gn_in"), sem("lraw_in"), [sem("bpad_in0"), sem("bpad_in1")]
    ada_sum, ada_ps, ada_out, bpad_use = sem("ada_sum"), sem("ada_ps"), sem("ada_out"), sem("bpad_used")
    csil_act, csil_rdy = sem("csil_act"), sem("csil_rdy")
    u_rdy = sem("u_rdy")
    out_rdy, out_act, out_dve, sig_rdy = sem("out_rdy"), sem("out_freed_act"), sem("out_freed_dve"), sem("sig_rdy")
    bias_ps, bvec_rdy, bvec_out, bias_in, bias_use = sem("bias_ps"), sem("bvec_rdy"), sem("bvec_out"), sem("bias_in"), sem("bias_used")
    bsel_in, brep_in = sem("bsel_in"), sem("brep_in")
    relb_one = sem("relb_one")
    gla_abs, gla_ln, gla_arg, gla_exp, gla_fac = sem("gla_abs"), sem("gla_ln"), sem("gla_arg"), sem("gla_exp"), sem("gla_fac")
    kt_ps, kt_sb, kv_ps, at_ps, st_sb, at_sb, o_ps, ssq_rdy, y_rdy = (sem(n) for n in (
        "kt_ps", "kt_sb", "kv_ps", "gatt_ps", "state_sb", "gatt_sb", "gla_o_ps", "ssq_rdy", "gla_y"))
    s_ps, s_sb, p_sb, pt_ps, pt_sb, pv_ps, og_rdy = (sem(n) for n in (
        "s_ps", "s_sb", "p_sb", "pt_ps", "pt_sb", "pv_ps", "og_rdy"))
    att_st = [sem("att_store0"), sem("att_store1")]
    att_ld, cm_m, cm_e, yatt_rdy, x1_in = sem("att_load"), sem("cm_max"), sem("cm_exp"), sem("yatt_rdy"), sem("x1_in")
    res_rdy, ln_in, u2_rdy, u2_st, u2T_ps, u2T_sb, lg_ps = (sem(n) for n in (
        "res_rdy", "ln_in", "u2_rdy", "u2_store", "u2T_ps", "u2T_sb", "logits_ps"))
    rt_ge, rt_gexp, rt_asg, rk_ps, slot_rdy, zero_rdy, ids_zero, ids_st, ids_ld, ids_ps, idx_rdy, tab_rdy = (sem(n) for n in (
        "rt_gargs", "rt_gexp", "rt_assign", "rank_ps", "slot_rdy", "zero_rdy", "ids_zero", "ids_store", "ids_load", "ids_ps", "idx_rdy", "tab_rdy"))
    wgi, wui, wdi = ([sem(f"{n}{i}") for i in range(2)] for n in ("w_gate_in", "w_up_in", "w_down_in"))
    m_up0 = sem("moe_up0_ps")
    m_hi, m_lo, x1_st, x1_back, x_hi, h_hi = (sem(n) for n in ("w_hi", "w_lo", "x1_store", "x1_back", "moe_x_hi", "moe_h_hi"))
    xg_in = [sem("xg_in0"), sem("xg_in1")]
    idxc_rdy, m_xt, m_xT, m_gate, m_sig, m_gs, m_up, m_h, m_hps, m_hT, m_y0, m_y, m_ya = (sem(n) for n in (
        "idxc_rdy", "moe_xt_ps", "moe_xT_sb", "moe_gate_ps", "moe_sig", "moe_gs", "moe_up_ps", "moe_h",
        "moe_ht_ps", "moe_hT_sb", "moe_y0_ps", "moe_y_ps", "moe_y_sb"))
    idxc_seen, y_zero = sem("idxc_seen"), sem("y_zero")
    y_st = [sem("y_store0"), sem("y_store1")]
    fin_in = [sem("fin_in0"), sem("fin_in1")]
    fin_use, fin_rdy, ln2_in = sem("fin_used"), sem("fin_rdy"), sem("ln2_in")
    out_st = [sem("out_store0"), sem("out_store1")]
    dve_own, act_own, pool_own = sem("dve_own"), sem("act_own"), sem("pool_own")

    own = {"dve": 0, "act": 0, "pool": 0}

    def kv_bank(c):
        half = GDV * (c // 2 % 2)
        return ps[:, 2 + 2 * (c % 2) + c // 4, half:half + GDV]

    def wait(eng, s, v):
        if not isinstance(v, int) or v > 0:
            eng.wait_ge(s, v)

    def freed_wait(pe, i):
        if i >= 2:
            e, v = freed(i - 2)
            pe.wait_ge(out_dve if e else out_act, v)

    def perm_in(v, g):
        r = STEP[g]
        return v if r == 1 else v.rearrange("p (l r) -> p r l", r=r)

    def perm_out(v, g):
        r = STEP[g]
        return v if r == 1 else v.rearrange("p (r l) -> p r l", r=r)

    def token_tile(k, g, t):
        if g == 0:
            return uT[:, k, P * t:P * t + P]
        return uT[:, k, :].rearrange("p (l r) -> p r l", r=4)[:, t, :]

    def group_of(n):
        c0 = items[n][2][1]
        return (c0 - QD) % 1536 // 512

    def pair_count(eng):
        return eng.value_load(tab_u[0:1, NCHUNK:NCHUNK + 1], min_val=NE // 2, max_val=(NE + MAX_EXTRA) // 2)

    block = ctx.enter_context(nc.Block())

    @block.sync
    def _(sp):
        sp.dma_start(ccol, c_col).then_inc(small_in, 16)
        sp.dma_start(cst[:, :], const).then_inc(small_in, 16)
        sp.dma_start(bgl, b_gla).then_inc(small_in, 16)
        sp.dma_start(wgg[:, :], w_gla_gate).then_inc(small_in, 16)
        sp.dma_start(brt, b_router.unsqueeze(0).broadcast_to([P, EG + NE])).then_inc(small_in, 16)

        def item(n):
            if before[n] is not None:
                m = before[n]
                if items[m][0] == "dve":
                    sp.wait_ge(ring_dve, dve_rank[m] + 1)
                else:
                    sp.wait_ge(out_rdy, LAST[m] + 1)
            kind = items[n][2][0]
            dst = ring[slot[n]][:, :, :]
            if kind == "pa":
                dst = dst.rearrange("p (k a) n -> p k (a n)", a=2)
            if kind == "ada":
                b = items[n][2][1]
                if b >= 2:
                    sp.wait_ge(bpad_use, b - 1)
                if b == 4:
                    sp.wait_ge(pv_ps, 2 * HPG)
                sp.wait_ge(zero_rdy, 1 if b < 4 else 2)
                sp.dma_start(bpad[b % 2][0:1, :], b_ada[:, 512 * b:512 * b + 512]).then_inc(bpad_in[b % 2], 16)
            sp.dma_start(dst, items[n][1]).then_inc(ring_in[slot[n]], 16)

        n_items = len(items)
        for n in range(n_items):
            item(n)
            if n == 1:
                sp.dma_start(x_in[:, :, :], x.rearrange("(t p) d -> p t d", p=P)).then_inc(x_load, 16)
                sp.dma_start(lra_w[:, :, :], cols(w_in, LRA, LOWRANK)).then_inc(lraw_in, 16)
                sp.dma_start(gn_b[:, :], gla_norm.broadcast_to([P, D])).then_inc(gn_in, 16)
        def load(dst, w, e, done):
            src = w[e] if isinstance(e, int) else w[bass.ds(e, 1)].rearrange("e k n -> (e k) n")
            sp.dma_start(dst[:, :, :], src.rearrange("(k p) n -> p k n", p=P)).then_inc(done, 16)

        def load_up(e, c):
            v = w_up[e] if isinstance(e, int) else w_up[bass.ds(e, 1)].rearrange("e k n -> (e k) n")
            v = v.rearrange("(k p) n -> p k n", p=P)
            for h, used in enumerate((m_up0, m_up)):
                wait(sp, used, c)
                sp.dma_start(wu[:, 4 * h:4 * h + 4, :], v[:, 4 * h:4 * h + 4, :]).then_inc(wui[h], 16)

        def load_down(e, c):
            v = w_down[e] if isinstance(e, int) else w_down[bass.ds(e, 1)].rearrange("e k n -> (e k) n")
            v = v.rearrange("(k p) n -> p k n", p=P)
            for h, used in enumerate((m_y0, m_y)):
                wait(sp, used, c)
                sp.dma_start(wd[:, :, 512 * h:512 * h + 512], v[:, :, 512 * h:512 * h + 512]).then_inc(wdi[h], 16)

        sp.wait_ge(out_rdy, len(outs))
        sp.wait_ge(ring_dve, 2 * N_MOD)
        load(wg[0], w_gate, 0, wgi[0])
        load_up(0, 0)
        sp.wait_ge(lg_ps, 1)
        sp.wait_ge(x1_st, 16 * NT)
        load_down(0, 0)
        load(wg[1], w_gate, 1, wgi[1])
        sp.wait_ge(m_gate, 1)
        load(wg[0], w_gate, 2, wgi[0])
        load_up(1, 1)
        load_down(1, 1)
        sp.wait_ge(tab_rdy, 1)
        with sp.Fori(1, pair_count(sp)) as i:
            for s in range(2):
                c = 2 * i + s
                e = sp.value_load(tab_u[0:1, bass.ds(c, 1)], min_val=0, max_val=NE - 1)
                e1 = sp.value_load(tab_u[0:1, bass.ds(c + 1, 1)], min_val=0, max_val=NE - 1)
                sp.wait_ge(m_gate, c)
                load(wg[1 - s], w_gate, e1, wgi[1 - s])
                load_up(e, c)
                load_down(e, c)

    @block.gpsimd
    def _(pool):
        def link(ins):
            own["pool"] += 1
            ins.then_inc(pool_own, 1)
            pool.wait_ge(pool_own, own["pool"])

        link(pool.memset(bpad[0][:, :], 0.0))
        link(pool.memset(bpad[1][:, :], 0.0))
        link(pool.memset(idsq[:, :], 0.0))
        link(pool.memset(relb[BUCKETS:BUCKETS + 1, :], 1.0))
        pool.sem_inc(relb_one, 1)
        pool.sem_inc(zero_rdy, 1)
        pool.dma_start(ids_d.rearrange("(i p) o -> i (p o)", p=P), idsq[:, :]).then_inc(ids_zero, 16)
        kz = KI[:, :, :, :].rearrange("p c i s -> p (c i s)")
        link(pool.memset(kz, 0.0))
        pool.dma_start(y_d[NE * C:(NE + MAX_EXTRA) * C, :].rearrange("(p i) d -> p (i d)", p=P)
                       .rearrange("p (a b) -> p a b", b=2048),
                       kz.unsqueeze(1).broadcast_to([P, MAX_EXTRA * D // 2048, 2048])).then_inc(y_zero, 16)
        pool.dma_start(relb[0:BUCKETS, :], rel_bias).then_inc(bsel_in, 16)
        pool.dma_start(bsel_sb[:, :], bias_sel).then_inc(bsel_in, 16)
        pool.wait_ge(bvec_rdy, 1)
        pool.dma_start(bvec_d, bvec_sb[:, :]).then_inc(bvec_out, 16)
        pool.wait_ge(bvec_out, 16)
        for g in range(GROUPS):
            pool.dma_start(brep_d[g].rearrange("q (h j) -> q h j", j=JB[g]),
                           bass.AP(bvec_d.tensor, JOFF[g], [[0, P], [NJ, HPG], [1, JB[g]]])).then_inc(brep_in, 16)
        pool.wait_ge(brep_in, 16 * GROUPS)

        def load_bias(g):
            if g == 1:
                pool.wait_ge(s_sb, HPG)
            if g == 2:
                pool.wait_ge(s_sb, 2 * HPG)
            n = JB[g] - P
            src = bass.AP(brep_d[g].tensor, P - 1, [[HPG * JB[g] - 1, P], [JB[g], HPG], [1, n]])
            pool.dma_start(bias[:, :, 0:n], src).then_inc(bias_in, 16)

        load_bias(0)
        load_bias(1)
        load_bias(2)
        pool.wait_ge(og_rdy, 2 * HPG)
        pool.dma_start(att_d[0].rearrange("(l r) c -> l r c", r=4),
                       Og[1][:, :, :, :].rearrange("p t h e -> p t (h e)")).then_inc(att_st[0], 16)
        pool.wait_ge(pv_ps, 2 * HPG)
        link(pool.memset(bpad[0][:, :], 0.0))
        link(pool.memset(bpad[1][:, :], 0.0))
        pool.sem_inc(zero_rdy, 1)
        pool.wait_ge(og_rdy, 3 * HPG)
        pool.dma_start(att_d[1].rearrange("(l r) c -> l r c", r=4),
                       Og[1][:, :, :, :].rearrange("p t h e -> p t (h e)")).then_inc(att_st[1], 16)
        for g in range(2):
            pool.wait_ge(att_st[g], 16)
            pool.dma_start((O1, O2)[g][:, :, :, :].rearrange("p t h e -> p t (h e)"),
                           att_d[g].rearrange("(t p) c -> p t c", p=P)).then_inc(att_ld, 16)
        pool.dma_start(x1[:, :, :], x.rearrange("(t p) d -> p t d", p=P)).then_inc(x1_in, 16)
        pool.wait_ge(yatt_rdy, 1)
        pool.wait_ge(out_rdy, [i for i, o in enumerate(outs) if o[0] == "yattT"][-1] + 1)
        pool.dma_start(ln_g[:, :], ln1_g.broadcast_to([P, D])).then_inc(ln_in, 16)
        pool.dma_start(ln_b[:, :], ln1_b.broadcast_to([P, D])).then_inc(ln_in, 16)
        pool.wait_ge(out_rdy, [i for i, o in enumerate(outs) if o[0] == "pa"][-1] + 1)
        pool.dma_start(wr_sb[:, :, :], w_router.rearrange("(k p) n -> p k n", p=P)).then_inc(ln_in, 16)
        for t in range(NT):
            pool.wait_ge(u2_rdy, t + 1)
            pool.dma_start(u2_d[P * t:P * t + P, :], u2[:, t, :]).then_inc(u2_st, 16)
            pool.dma_start(x1_d[P * t:P * t + P, :], x1[:, t, :]).then_inc(x1_st, 16)
        pool.wait_ge(slot_rdy, 1)
        pool.wait_ge(ids_zero, 16)
        for n in range(2 * NT):
            pool.indirect_dma_start(ids_d, bass.IndirectOffsetOnAxis(ap=slot_u[:, n:n + 1], axis=0),
                                    cst[:, TOKID + n % NT:TOKID + n % NT + 1], None).then_inc(ids_st, 16)
        pool.wait_ge(ids_st, 32 * NT)
        pool.dma_start(idsq[:, :], ids_d.rearrange("(i p) o -> i (p o)", p=P)).then_inc(ids_ld, 16)
        pool.wait_ge(u2_st, 16 * NT)
        pool.wait_ge(idx_rdy, 1)

        def gather(c, s, n):
            wait(pool, m_xt, c - 1)
            pool.tensor_copy(idxc[s], idx_u[:, bass.ds(c, 1)]).then_inc(idxc_rdy, 1)
            pool.wait_ge(idxc_rdy, c + 1)
            pool.sem_inc(idxc_seen, 1)
            pool.indirect_dma_start(xg[s][:, :], None, u2_d,
                                    bass.IndirectOffsetOnAxis(ap=idxc[s], axis=0)).then_inc(xg_in[s], 16)

        gather(0, 0, 0)
        gather(1, 1, 1)
        gather(2, 0, 2)
        with pool.Fori(1, pair_count(pool)) as i:
            gather(2 * i + 1, 1, None)
            gather(2 * i + 2, 0, None)
        npair = pair_count(pool)
        for s in range(2):
            pool.wait_ge(y_st[s], npair * 16)
            pool.sem_inc(idxc_seen, 1)
        pool.dma_start(x1[:, :, :], x1_d.rearrange("(t p) d -> p t d", p=P)).then_inc(x1_back, 16)
        for t in range(NT):
            if t >= 2:
                pool.wait_ge(fin_use, t - 1)
            for k, dst in ((0, ya), (1, yc)):
                pool.indirect_dma_start(dst[t % 2][:, :], None, y_d,
                                        bass.IndirectOffsetOnAxis(ap=slot_u[:, k * NT + t:k * NT + t + 1], axis=0)
                                        ).then_inc(fin_in[t % 2], 16)

    @block.tensor
    def _(pe):
        def tile_product(dst, lhs, rhs, n, done=None):
            for k in range(n):
                last = pe.matmul(dst, lhs(k), rhs(k), start=(k == 0), stop=(k == n - 1))
            if done is not None:
                last.then_inc(done, 1)
            return last

        pe.wait_ge(relb_one, 1)
        pe.wait_ge(bsel_in, 32)
        for g in range(GROUPS):
            dst = bank(2)[0:HPG, 0:JB[0]] if g == 0 else bank(3)[0:HPG, JOFF[g] - JOFF[1]:JOFF[g] - JOFF[1] + JB[g]]
            last = pe.matmul(dst, relb[:, HPG * g:HPG * g + HPG], bsel_sb[:, JOFF[g]:JOFF[g] + JB[g]],
                             start=True, stop=True)
        last.then_inc(bias_ps, 1)
        pe.wait_ge(small_in, 80)

        def out_step(i):
            kind, q, n = outs[i]
            dst = bank(i % 2)
            freed_wait(pe, i)
            if n is not None:
                pe.wait_ge(ring_in[slot[n]], 16 * (rank[n] + 1))
            w = ring[slot[n]] if n is not None else None
            qc = slice(P * q, P * q + P)
            if kind == "uT":
                pe.wait_ge(u_rdy, NT)
                for t in range(NT):
                    last = pe.transpose(dst[:, P * t:P * t + P], u_nat[:, t, P * q:P * q + P], ident)
            elif kind == "yT":
                pe.wait_ge(y_rdy, GH)
                for t in range(NT):
                    last = pe.transpose(dst[:, P * t:P * t + P], va[:, t, P * q:P * q + P], ident)
            elif kind == "yattT":
                pe.wait_ge(yatt_rdy, 1)
                yv = yatt[:, :, :, :].rearrange("p t h e -> p t (h e)")
                for t in range(NT):
                    last = pe.transpose(dst[:, P * t:P * t + P], yv[:, t, P * q:P * q + P], ident)
            elif kind == "lra":
                pe.wait_ge(lraw_in, 16)
                pe.wait_ge(out_act, KD)
                last = tile_product(dst[0:LOWRANK, :], lambda k: lra_w[:, k, :], lambda k: uT[:, k, :], KD)
            elif kind == "gp":
                pe.wait_ge(out_act, freed([j for j, o in enumerate(outs) if o[0] == "lra"][0])[1])
                last = pe.matmul(dst, wgg[:, qc], lraT[:, :], start=True, stop=True)
            elif kind in ("qa", "ka", "qd", "kd", "ga", "gd"):
                last = tile_product(dst, lambda k: w[:, k, qc], lambda k: uT[:, k, :], KD)
            elif kind in ("va", "ra"):
                last = tile_product(dst, lambda k: uT[:, k, qc], lambda k: w[:, k, :], KD)
            elif kind == "vd":
                g = group_of(n)
                last = tile_product(dst, lambda k: token_tile(k, g, q), lambda k: w[:, k, :], KD)
            elif kind == "pg":
                if q == 0:
                    pe.wait_ge(out_act, freed(max(j for j, o in enumerate(outs) if o[0] == "yT"))[1])
                qq = slice(P * (q % 4), P * (q % 4) + P)
                last = tile_product(dst, lambda k: w[:, k, qq], lambda k: yglaT[:, k, :], KD)
            elif kind == "pa":
                if q == 0:
                    pe.wait_ge(out_act, freed(max(j for j, o in enumerate(outs) if o[0] == "yattT"))[1])
                wv = w[:, :, :].rearrange("p (k a) n -> p k (a n)", a=2)
                last = tile_product(dst, lambda k: wv[:, k, qc], lambda k: yattT[:, k, :], 4)
            else:
                t = q // 2
                if q == 0:
                    pe.wait_ge(out_dve, freed(max(j for j, o in enumerate(outs) if o[0] == "pa"))[1])
                last = tile_product(dst, lambda k: mT[:, k, P * t:P * t + P], lambda k: w[:, k, :], KD)
            last.then_inc(out_rdy, 1)
        for kind, a in steps:
            if kind == "ada":
                pe.wait_ge(ada_sum, a + 1)
                if a >= 2:
                    pe.wait_ge(ada_out, a - 1)
                if a == 4:
                    pe.wait_ge(y_rdy, GH)
                if a >= 1:
                    pe.wait_ge(ada_out, a)
                pe.matmul(bank(7), ones, acc[a % 2][:, :], start=True, stop=True).then_inc(ada_ps, 1)
            elif kind == "z":
                out_step(a)
            elif kind == "gla_kt":
                pe.wait_ge(gla_fac, a + 1)
                if a:
                    pe.wait_ge(y_rdy, a)
                for t in range(NT):
                    last = pe.transpose(bank(6)[:, P * t:P * t + P], t2[:, P * t:P * t + P], ident)
                last.then_inc(kt_ps, 1)
            elif kind == "gla_kv":
                if a == 0:
                    pe.wait_ge(bvec_rdy, 1)
                    pe.wait_ge(out_act, freed(max(j for j, o in enumerate(outs) if o[0] == "va"))[1])
                for c in range(NCH):
                    p0 = CHUNK * (c % 2)
                    for i in range(NSUB):
                        q0 = CHUNK * c + SUB * i
                        last = pe.matmul(bank(7)[p0:p0 + CHUNK, CHUNK * (c // 2) + SUB * i:CHUNK * (c // 2) + SUB * i + SUB],
                                         KI[:, c, i, :], t1[:, q0:q0 + SUB], start=True, stop=True)
                last.then_inc(at_ps, 1)
                pe.wait_ge(kt_sb, a + 1)
                if a:
                    pe.wait_ge(st_sb, a)
                for c in range(NCH - 1):
                    p0 = CHUNK * (c % 2)
                    last = pe.matmul(kv_bank(c), kdN[p0:p0 + CHUNK, c // 2, :],
                                     va[p0:p0 + CHUNK, c // 2, GDV * a:GDV * a + GDV], start=True, stop=True)
                last.then_inc(kv_ps, 1)
            elif kind == "gla_o":
                pe.wait_ge(st_sb, a + 1)
                pe.wait_ge(at_sb, a + 1)
                for c in range(NCH):
                    p0 = CHUNK * (c % 2)
                    dst = ps[p0:p0 + CHUNK, 6 + c // 4, GDV * (c // 2 % 2):GDV * (c // 2 % 2) + GDV]
                    last = pe.matmul(dst, attT[p0:p0 + CHUNK, c // 2, :],
                                     va[p0:p0 + CHUNK, c // 2, GDV * a:GDV * a + GDV], start=True, stop=(c == 0))
                    if c:
                        last = pe.matmul(dst, t3[:, CHUNK * c:CHUNK * c + CHUNK], St[:, c, :], start=False, stop=True)
                last.then_inc(o_ps, 1)
            elif kind == "S":
                g, j = a // HPG, a % HPG
                if a == 0:
                    pe.wait_ge(st_sb, GH)
                if a:
                    pe.wait_ge(s_sb, a)
                if j == 0:
                    last_v = max(i for i, o in enumerate(outs) if o[0] == "vd" and group_of(o[2]) == g)
                    pe.wait_ge(out_act, freed(last_v)[1])
                f, p0 = j // 2, DH * (j % 2)
                q, k = qg[g % 2], kg[g % 2]
                for t in range(NT):
                    lhs = q[p0:p0 + DH, f, P * t:P * t + P]
                    if g == 0:
                        k0 = 0 if t else 1
                        dst = ps[:, 2 + t // 2, 256 * (t % 2) + P * k0:256 * (t % 2) + 256]
                        rhs = k[p0:p0 + DH, f, P * (t - 1 + k0):P * t + P]
                    else:
                        dst = ps[:, 2, P * t:P * t + P]
                        rhs = k[p0:p0 + DH, f, P * t:P * t + P]
                    last = pe.matmul(dst, lhs, rhs, start=True, stop=True)
                last.then_inc(s_ps, 1)
            elif kind == "T":
                g = a // HPG
                pe.wait_ge(p_sb, a + 1)
                if a:
                    pe.wait_ge(pt_sb, a)
                for t in range(NT):
                    for half in ((0, 1) if g == 0 else (0,)):
                        if g == 0 and t == 0 and half == 0:
                            continue
                        m = 2 * t + half if g == 0 else t
                        last = pe.transpose(ps[:, 4 + m // 4, P * (m % 4):P * (m % 4) + P],
                                            Pr[a % 2][:, t, P * half:P * half + P] if g == 0 else
                                            Pr[a % 2][:, t, 0:P], ident)
                last.then_inc(pt_ps, 1)
            elif kind == "PV":
                g, j = a // HPG, a % HPG
                pe.wait_ge(pt_sb, a + 1)
                if a:
                    pe.wait_ge(og_rdy, a)
                else:
                    pe.wait_ge(y_rdy, GH)
                v = vg[g % 2]
                for t in range(NT):
                    dst = bank(6)[:, DH * t:DH * t + DH]
                    if g == 0 and t:
                        pe.matmul(dst, PT[a % 2][:, 2 * t, :], v[:, t - 1, DH * j:DH * j + DH], start=True, stop=False)
                    m = 2 * t + 1 if g == 0 else t
                    last = pe.matmul(dst, PT[a % 2][:, m, :], v[:, t, DH * j:DH * j + DH],
                                     start=not (g == 0 and t), stop=True)
                last.then_inc(pv_ps, 1)

        for k in range(KD):
            pe.wait_ge(u2_rdy, NT)
            if k >= 2:
                pe.wait_ge(u2T_sb, k - 1)
            for t in range(NT):
                last = pe.transpose(bank(2 + k % 2)[:, P * t:P * t + P], u2[:, t, P * k:P * k + P], ident)
            last.then_inc(u2T_ps, 1)
        pe.wait_ge(u2T_sb, KD)
        pe.wait_ge(ln_in, 48)
        for t in range(NT):
            last = tile_product(bank(4)[:, 64 * t:64 * t + EG + NE], lambda k: u2T[:, k, P * t:P * t + P],
                                lambda k: wr_sb[:, k, :], KD)
        last.then_inc(lg_ps, 1)
        pe.wait_ge(rt_asg, 1)
        for t in range(NT):
            for tt in range(t + 1):
                pe.matmul(bank(5)[:, NE * t:NE * t + NE], cst[:, TRI:TRI + P] if tt == t else ones,
                          rt[:, 0, tt, :], start=(tt == 0), stop=(tt == t))
        for tt in range(NT):
            last = pe.matmul(bank(5)[:, NE * NT:NE * NT + NE], ones, rt[:, 0, tt, :], start=(tt == 0), stop=(tt == NT - 1))
        last.then_inc(rk_ps, 1)
        pe.wait_ge(ids_ld, 16)
        pe.transpose(bank(6)[:, 0:NCHUNK], idsq[:, :], cst[0:NCHUNK, IDENT:IDENT + NCHUNK]).then_inc(ids_ps, 1)

        def x_transposes(c, s, loads):
            pe.wait_ge(xg_in[s], 16 * loads)
            wait(pe, m_xT, c)
            for k in range(KD):
                last = pe.transpose(ps[:, 2 + k // 4, P * (k % 4):P * (k % 4) + P], xg[s][:, P * k:P * k + P], ident)
            last.then_inc(m_xt, 1)

        def split_product(dst, a_hi, a_lo, w_hi, w_lo, n, done, half_done=None):
            for k in range(n):
                pe.matmul(dst, a_hi[:, k, :], w_hi(k), start=(k == 0), stop=False)
                pe.matmul(dst, a_hi[:, k, :], w_lo(k), start=False, stop=False)
                last = pe.matmul(dst, a_lo[:, k, :], w_hi(k), start=False, stop=(k == n - 1))
                if half_done is not None and k == n // 2 - 1:
                    last.then_inc(half_done, 1)
            last.then_inc(done, 1)

        def chunk(i, s):
            c = 2 * i + s
            pe.wait_ge(m_lo, 6 * c + 2)
            pe.wait_ge(m_xT, c + 1)
            wait(pe, m_gs, c)
            split_product(bank(0), xT_hi, xT_lo, lambda k: wg_hi[s][:, k, :], lambda k: wg_lo[s][:, k, :], KD, m_gate)
            pe.wait_ge(m_lo, 6 * c + 4)
            wait(pe, m_h, c)
            split_product(bank(1), xT_hi, xT_lo, lambda k: wu_hi[:, k, :], lambda k: wu_lo[:, k, :], KD, m_up, m_up0)
            x_transposes(c + 1, 1 - s, i + 1 + s)
            pe.wait_ge(m_h, c + 1)
            for f in range(FD):
                last = pe.transpose(bank(4)[:, P * f:P * f + P], hb[:, P * f:P * f + P], ident)
            last.then_inc(m_hps, 1)
            pe.wait_ge(m_lo, 6 * c + 6)
            pe.wait_ge(m_hT, c + 1)
            wait(pe, m_ya, 2 * c)
            split_product(bank(5), hT_hi, hT_lo, lambda k: wd_hi[:, k, 0:512], lambda k: wd_lo[:, k, 0:512], FD, m_y0)
            split_product(bank(6), hT_hi, hT_lo, lambda k: wd_hi[:, k, 512:D], lambda k: wd_lo[:, k, 512:D], FD, m_y)

        pe.wait_ge(tab_rdy, 1)
        x_transposes(0, 0, 1)
        chunk(0, 0)
        chunk(0, 1)
        with pe.Fori(1, pair_count(pe)) as i:
            chunk(i, 0)
            chunk(i, 1)

    @block.scalar
    def _(act):
        def link(ins):
            own["act"] += 1
            ins.then_inc(act_own, 1)
            act.wait_ge(act_own, own["act"])

        act.wait_ge(small_in, 80)
        act.activation(csil, ccol, ACT.Sigmoid).then_inc(csil_act, 1)
        act.wait_ge(bias_ps, 1)
        act.copy(bvec_sb[:, 0:JB[0]], bank(2)[0:HPG, 0:JB[0]])
        link(act.copy(bvec_sb[:, JB[0]:NJ], bank(3)[0:HPG, 0:NJ - JB[0]]))
        act.sem_inc(bvec_rdy, 1)

        def evac(i):
            kind, q, n = outs[i]
            src = bank(i % 2)
            if kind in DVE_OUT and kind != "ra":
                return
            act.wait_ge(out_rdy, i + 1)
            if kind == "ra":
                m = sum(o[0] == "ra" for o in outs[:i])
                if m == 0:
                    act.wait_ge(bvec_out, 16)
                if m:
                    act.wait_ge(out_dve, freed([j for j, o in enumerate(outs) if o[0] == "ra"][m - 1])[1])
                act.activation(sig_t[:, :], src, ACT.Sigmoid).then_inc(sig_rdy, 1)
                return
            if kind == "uT":
                last = act.copy(uT[:, q, :], src)
            elif kind == "yT":
                last = act.copy(yglaT[:, q, :], src)
            elif kind == "yattT":
                last = act.copy(yattT[:, q, :], src)
            elif kind == "lra":
                last = act.copy(lraT[:, :], src[0:LOWRANK, :])
            elif kind == "qa":
                last = act.mul(qaT[:, q, :], src, GDK ** -0.5)
            elif kind == "ka":
                last = act.copy(kaT[:, q, :], src)
            elif kind == "va":
                c0 = items[n][2][1] - VA
                last = act.copy(va[:, q, c0:c0 + 512], src)
            elif kind in ("qd", "kd", "vd"):
                g = group_of(n)
                if kind == "qd" and q == 0 and g == 2:
                    act.wait_ge(pv_ps, HPG)
                if kind == "vd" and q == 0 and g == 0:
                    act.wait_ge(ids_zero, 16)
                if kind == "vd":
                    last = act.copy(vg[g % 2][:, q, :], src)
                else:
                    dst = (qg if kind == "qd" else kg)[g % 2][:, q, :]
                    last = act.copy(perm_out(dst, g), perm_in(src, g))
            else:
                c0 = (items[n][2][1] - (GA if kind == "ga" else GD)) // P
                last = act.activation((sga if kind == "ga" else sgd)[:, c0 + q, :], src, ACT.Sigmoid)
            last.then_inc(out_act, 1)

        for kind, a in steps:
            if kind == "z":
                evac(a)
            elif kind == "gla_args":
                act.wait_ge(gla_abs, a + 1)
                link(act.activation(t2[:, :], t2[:, :], ACT.Exp, scale=-1.0))
                act.activation(t2[:, :], t2[:, :], ACT.Ln, bias=1.0).then_inc(gla_ln, 1)
                act.wait_ge(gla_arg, a + 1)
                act.activation(t1[:, :], t1[:, :], ACT.Exp, scale=1.0 / TAU)
                act.activation(t2[:, :], t2[:, :], ACT.Exp, scale=1.0 / TAU)
                act.activation(t3[:, :], Bc[:, :], ACT.Exp, scale=1.0 / TAU)
                act.activation(Dl, Bc[:, :].rearrange("p (c s) -> p c s", s=CHUNK)[:, :, CHUNK - 1], ACT.Exp, scale=1.0 / TAU)
                ki = KI[:, :, :, :].rearrange("p c i s -> p (c i s)")
                act.activation(ki, ki, ACT.Exp, scale=1.0 / TAU).then_inc(gla_exp, 1)
            elif kind == "gla_o":
                act.wait_ge(o_ps, a + 1)
                for t in range(NT):
                    link(act.activation(sq_junk[:, :], ps[:, 6 + t // 2, GDV * (t % 2):GDV * (t % 2) + GDV], ACT.Square,
                                        accum_out=ssq[:, t:t + 1]))
                act.sem_inc(ssq_rdy, 1)
            elif kind == "S":
                g, j = a // HPG, a % HPG
                act.wait_ge(s_sb, a + 1)
                if a >= 2:
                    act.wait_ge(pt_ps, a - 1)
                if j == 0 and g == 2:
                    act.wait_ge(att_st[0], 16)
                og = Og[0 if g == 0 else 1]
                for t in range(NT):
                    w0, w1 = (0 if g == 0 and t else P if g == 0 else 0), (256 if g == 0 else P)
                    last = act.activation(Pr[a % 2][:, t, w0:w1], Ssb[a % 2][:, t, w0:w1], ACT.Exp,
                                          bias=nmx[a % 2][:, t:t + 1], accum_out=og[:, t, j, DH + 1:DH + 2])
                last.then_inc(p_sb, 1)
            elif kind == "PV":
                g, j = a // HPG, a % HPG
                act.wait_ge(pv_ps, a + 1)
                og = Og[0 if g == 0 else 1]
                link(act.copy(og[:, :, j, 0:DH], bank(6)[:, 0:NT * DH].rearrange("p (t e) -> p t e", e=DH)))
                act.sem_inc(og_rdy, 1)
            elif kind == "combine":
                act.wait_ge(cm_m, 1)
                act.activation(cmb[:, 0:3, :], cmb[:, 0:3, :], ACT.Exp).then_inc(cm_e, 1)

        for k in range(KD):
            act.wait_ge(u2T_ps, k + 1)
            act.copy(u2T[:, k, :], bank(2 + k % 2)).then_inc(u2T_sb, 1)
        act.wait_ge(rt_ge, 1)
        act.activation(rt_w[:, 0:16], rt_w[:, 0:16], ACT.Exp).then_inc(rt_gexp, 1)
        act.wait_ge(rt_ge, 2)
        act.activation(rt_w[:, 32:36], rt_w[:, 32:36], ACT.Exp).then_inc(rt_gexp, 1)

        def x_split(c):
            act.wait_ge(m_xt, c + 1)
            wait(act, m_up, c)
            for half in range(2):
                last = act.copy(xT_hi[:, 4 * half:4 * half + 4, :], bank(2 + half).rearrange("p (k c) -> p k c", c=C))
            last.then_inc(x_hi, 1)

        def halves(w, by_columns):
            if by_columns:
                return [w[:, :, 512 * h:512 * h + 512] for h in range(2)]
            return [w[:, 4 * h:4 * h + 4, :] for h in range(2)]

        def w_split(raw, hi, arrived, n, used, m, by_columns=False):
            for h, (a, b) in enumerate(zip(halves(raw, by_columns), halves(hi, by_columns))):
                act.wait_ge(arrived[h], n)
                wait(act, used[h], m)
                act.copy(b, a).then_inc(m_hi, 1)

        def y_store(c, s, before):
            act.wait_ge(m_y, c + 1)
            wait(act, y_st[s], 16 * before)
            act.copy(yb[s][:, 0:512], bank(5)).then_inc(m_ya, 1)
            act.copy(yb[s][:, 512:D], bank(6)).then_inc(m_ya, 1)
            act.wait_ge(m_ya, 2 * c + 2)
            act.dma_start(y_d[bass.ds(c * C, C), :], yb[s][:, :]).then_inc(y_st[s], 16)

        def chunk(i, s, stored):
            c = 2 * i + s
            w_split(wu, wu_hi, wui, 16 * (c + 1), (m_up0, m_up), c)
            if not isinstance(i, int) or c > 0:
                y_store(c - 1, 1 - s, stored)
            act.wait_ge(m_gate, c + 1)
            wait(act, m_gs, c)
            act.activation(sgb[:, :], bank(0), ACT.Sigmoid).then_inc(m_sig, 1)
            w_split(wd, wd_hi, wdi, 16 * (c + 1), (m_y0, m_y), c, by_columns=True)
            act.wait_ge(m_hps, c + 1)
            wait(act, m_y, c)
            act.copy(hT_hi[:, :, :], bank(4).rearrange("p (f c) -> p f c", c=C)).then_inc(h_hi, 1)
            x_split(c + 1)
            w_split(wg[1 - s], wg_hi[1 - s], [wgi[1 - s]] * 2, 16 * (i + 1 + s), (m_gate, m_gate), c)

        act.wait_ge(u2_st, 16 * NT)
        act.wait_ge(tab_rdy, 1)
        w_split(wg[0], wg_hi[0], [wgi[0]] * 2, 16, (m_gate, m_gate), 0)
        x_split(0)
        for i in range(2):
            chunk(i, 0, i - 1)
            chunk(i, 1, i)
        last_pair = act.value_load(tab_u[0:1, NCHUNK + 1:NCHUNK + 2], min_val=NE // 2 - 1, max_val=(NE + MAX_EXTRA) // 2 - 1)
        with act.Fori(1, last_pair) as j:
            for s in range(2):
                chunk(j + 1, s, j + s)
        y_store(2 * last_pair + 1, 1, last_pair)
        act.dma_start(ln2gb[:, 0, :], ln2_g.broadcast_to([P, D])).then_inc(ln2_in, 16)
        act.dma_start(ln2gb[:, 1, :], ln2_b.broadcast_to([P, D])).then_inc(ln2_in, 16)
        for t in range(NT):
            act.wait_ge(fin_rdy, t + 1)
            act.dma_start(out[P * t:P * t + P, :], r2[t % 2][:, :]).then_inc(out_st[t % 2], 16)
        for s in range(2):
            act.wait_ge(out_st[s], 16 * NT // 2)

    @block.vector
    def _(dve):
        def link(ins):
            own["dve"] += 1
            ins.then_inc(dve_own, 1)
            dve.wait_ge(dve_own, own["dve"])

        def bc(ap, axis, n):
            v = ap.unsqueeze(axis)
            shape = list(v.shape)
            shape[axis] = n
            return v.broadcast_to(shape)

        dve.wait_ge(csil_act, 1)
        link(dve.tensor_tensor(csil, csil, ccol, ALU.mult))

        def ada_sum_up(b):
            n = ada_item[b]
            dve.wait_ge(ring_in[slot[n]], 16 * (rank[n] + 1))
            dve.wait_ge(bpad_in[b % 2], 16 * (b // 2 + 1))
            if b >= 2:
                dve.wait_ge(ada_ps, b - 1)
            a = acc[b % 2]
            for k in range(KD):
                ins = dve.scalar_tensor_tensor(out=a[:, :], in0=ring[slot[n]][:, k, :], scalar=csil[:, k:k + 1],
                                               in1=(bpad[b % 2] if k == 0 else a)[:, :], op0=ALU.mult, op1=ALU.add)
                if k == 0:
                    ins.then_inc(bpad_use, 1)
                    dve.wait_ge(bpad_use, b + 1)
                elif k < KD - 1:
                    link(ins)
                else:
                    ins.then_inc(ada_sum, 1)
                    dve.wait_ge(ada_sum, b + 1)
            dve.sem_inc(ring_dve, 1)

        def ada_move(b):
            dve.wait_ge(ada_ps, b + 1)
            mod, half = b // 2, slice(512 * (b % 2), 512 * (b % 2) + 512)
            dst = mods_a[:, mod, half] if mod < 2 else mods[:, mod - 2, half]
            add = 1.0 if mod in (1, 4) else 0.0
            dve.tensor_scalar(dst, bank(7), add, None, ALU.add).then_inc(ada_out, 1)

        def evac(i):
            kind, q, n = outs[i]
            src = bank(i % 2)
            if kind not in DVE_OUT or kind == "gp":
                return
            dve.wait_ge(out_rdy, i + 1)
            if kind == "ra":
                m = sum(o[0] == "ra" for o in outs[:i])
                if m == 0:
                    dve.wait_ge(gn_in, 16)
                c0 = items[n][2][1] - RA
                dve.wait_ge(sig_rdy, m + 1)
                d = sr[:, q, c0:c0 + 512]
                link(dve.tensor_tensor(d, src, sig_t[:, :], ALU.mult))
                link(dve.tensor_tensor(d, d, gn_b[:, c0:c0 + 512], ALU.mult))
                dve.sem_inc(out_dve, 1)
            elif kind == "pg":
                if q == 0:
                    dve.wait_ge(out_act, freed(max(j for j, o in enumerate(outs) if o[0] == "gd"))[1])
                dve.tensor_tensor(mT[:, q, :], src, sga[:, q, :], ALU.mult).then_inc(out_dve, 1)
            elif kind == "pa":
                link(dve.tensor_tensor(sgd[:, q, :], src, sgd[:, q, :], ALU.mult))
                link(dve.tensor_tensor(mT[:, q, :], mT[:, q, :], sgd[:, q, :], ALU.add))
                dve.sem_inc(out_dve, 1)
            else:
                t, half = q // 2, q % 2
                hs = slice(512 * half, 512 * half + 512)
                if q == 0:
                    dve.wait_ge(x1_in, 16)
                    dve.wait_ge(ada_out, 10)
                    dve.wait_ge(ln_in, 48)
                link(dve.tensor_tensor(lnt[0][:, hs], src, mods[:, 0, hs], ALU.mult))
                link(dve.scalar_tensor_tensor(out=x1[:, t, hs], in0=x1[:, t, hs], scalar=ALPHA, in1=lnt[0][:, hs],
                                              op0=ALU.mult, op1=ALU.add))
                dve.sem_inc(out_dve, 1)
                if half:
                    norm_rows(x1[:, t, :], ln_g[:, :], ln_b[:, :])
                    link(dve.tensor_tensor(u2[:, t, :], x1[:, t, :], mods[:, 2, :], ALU.mult))
                    dve.tensor_tensor(u2[:, t, :], u2[:, t, :], mods[:, 1, :], ALU.add).then_inc(u2_rdy, 1)

        def rsqrt(r, v, t):
            link(dve.tensor_scalar(r.bitcast(u32), v.bitcast(u32), -0.5, float(0x5F3759DF), ALU.mult, ALU.add))
            for _ in range(4):
                link(dve.scalar_tensor_tensor(out=t, in0=r, scalar=-0.5, in1=r, op0=ALU.mult, op1=ALU.mult))
                link(dve.tensor_tensor(t, t, v, ALU.mult))
                link(dve.scalar_tensor_tensor(out=r, in0=t, scalar=1.5, in1=r, op0=ALU.add, op1=ALU.mult))

        def norm_rows(v, g, b):
            dve.bn_stats(bnst[:, 0:6], v[:, 0:512])
            link(dve.bn_stats(bnst[:, 6:12], v[:, 512:1024]))
            link(dve.bn_aggr(bnag, bnst))
            link(dve.tensor_scalar(bnag[:, 1:2], bnag[:, 1:2], EPS, None, ALU.add))
            rsqrt(lrs, bnag[:, 1:2], rs_t[:, 0:1])
            link(dve.tensor_scalar(v, v, bnag[:, 0:1], lrs, ALU.subtract, ALU.mult))
            link(dve.tensor_tensor(v, v, g, ALU.mult))
            link(dve.tensor_tensor(v, v, b, ALU.add))

        for b in range(4):
            ada_sum_up(b)
            if b:
                ada_move(b - 1)
        ada_move(3)
        dve.wait_ge(ada_out, 4)
        dve.wait_ge(x_load, 16)
        for t in range(NT):
            link(dve.tensor_tensor(u_nat[:, t, :], x_in[:, t, :], mods_a[:, 1, :], ALU.mult))
            dve.tensor_tensor(u_nat[:, t, :], u_nat[:, t, :], mods_a[:, 0, :], ALU.add).then_inc(u_rdy, 1)

        Bb = Bc[:, :].rearrange("p (m s) -> p m s", s=SUB)
        Bch = Bc[:, :].rearrange("p (c s) -> p c s", s=CHUNK)
        Bref = Bc[:, :].rearrange("p (c i s) -> p c i s", c=NCH, i=NSUB)[:, :, :, SUB // 2 - 1]
        for kind, a in steps[4:]:
            if kind == "z":
                evac(a)
            elif kind == "gla_args":
                gp = [i for i, o in enumerate(outs) if o[0] == "gp" and o[1] == a][0]
                dve.wait_ge(out_rdy, gp + 1)
                if a == 0:
                    dve.wait_ge(bvec_out, 16)
                    dve.wait_ge(y_zero, 16)
                    dve.wait_ge(out_act, freed(max(j for j, o in enumerate(outs) if o[0] == "ka"))[1])
                if a:
                    dve.wait_ge(o_ps, a)
                link(dve.tensor_scalar(t1[:, :], bank(gp % 2), bgl[:, a:a + 1], None, ALU.add))
                dve.sem_inc(out_dve, 1)
                dve.scalar_tensor_tensor(out=t2[:, :], in0=t1[:, :], scalar=-1.0, in1=t1[:, :],
                                         op0=ALU.mult, op1=ALU.max).then_inc(gla_abs, 1)
                dve.wait_ge(gla_ln, a + 1)
                link(dve.scalar_tensor_tensor(out=t1[:, :], in0=t1[:, :], scalar=0.0, in1=t2[:, :],
                                              op0=ALU.min, op1=ALU.subtract))
                link(dve.tensor_tensor_scan(Bc[:, :], cst[:, RESET:RESET + S], t1[:, :], 0.0, ALU.mult, ALU.add))
                dve.tensor_tensor(KI[:, :, :, :], bc(Bref, 3, CHUNK), bc(Bch, 2, NSUB), ALU.subtract)
                dve.tensor_tensor(t1[:, :].rearrange("p (m s) -> p m s", s=SUB), Bb,
                                  bc(Bb[:, :, SUB // 2 - 1], 2, SUB), ALU.subtract)
                link(dve.tensor_tensor(t2[:, :].rearrange("p (c s) -> p c s", s=CHUNK), bc(Bch[:, :, CHUNK - 1], 2, CHUNK),
                                       Bch, ALU.subtract))
                ki = KI[:, :, :, :].rearrange("p c i s -> p (c i s)")
                dve.tensor_scalar(ki, ki, CLAMP * TAU, None, ALU.min)
                dve.tensor_scalar(t1[:, :], t1[:, :], CLAMP * TAU, None, ALU.min).then_inc(gla_arg, 1)
                dve.wait_ge(gla_exp, a + 1)
                kc = kaT[:, a, :].rearrange("p (c s) -> p c s", s=CHUNK)
                dve.tensor_tensor(t1[:, :], t1[:, :], qaT[:, a, :], ALU.mult)
                dve.tensor_tensor(t2[:, :], t2[:, :], kaT[:, a, :], ALU.mult)
                dve.tensor_tensor(t3[:, :], t3[:, :], qaT[:, a, :], ALU.mult)
                dve.tensor_tensor(KI[:, :, :, :], KI[:, :, :, :], bc(kc, 2, NSUB), ALU.mult).then_inc(gla_fac, 1)
            elif kind == "gla_kt":
                dve.wait_ge(kt_ps, a + 1)
                dve.tensor_copy(kdN[:, :, :], bank(6).rearrange("p (t k) -> p t k", k=P)).then_inc(kt_sb, 1)
            elif kind == "gla_kv":
                dve.wait_ge(at_ps, a + 1)
                dve.tensor_tensor(attT[:, :, :], bank(7)[:, 0:NT * CHUNK].rearrange("p (t s) -> p t s", s=CHUNK),
                                  bc(cst[:, GMASK:GMASK + CHUNK], 1, NT), ALU.mult).then_inc(at_sb, 1)
                dve.wait_ge(kv_ps, a + 1)
                link(dve.tensor_copy(St[:, 1, :], kv_bank(0)))
                for c in range(1, NCH - 1):
                    ins = dve.scalar_tensor_tensor(out=St[:, c + 1, :], in0=St[:, c, :], scalar=Dl[:, c:c + 1],
                                                   in1=kv_bank(c),
                                                   op0=ALU.mult, op1=ALU.add)
                    if c < NCH - 2:
                        link(ins)
                ins.then_inc(st_sb, 1)
            elif kind == "gla_o":
                dve.wait_ge(ssq_rdy, a + 1)
                link(dve.tensor_scalar(ssq, ssq, 1.0 / GDV, EPS, ALU.mult, ALU.add))
                rsqrt(rstd, ssq, rs_t)
                for t in range(NT):
                    ins = dve.scalar_tensor_tensor(out=va[:, t, GDV * a:GDV * a + GDV],
                                                   in0=ps[:, 6 + t // 2, GDV * (t % 2):GDV * (t % 2) + GDV],
                                                   scalar=rstd[:, t:t + 1], in1=sr[:, t, GDV * a:GDV * a + GDV],
                                                   op0=ALU.mult, op1=ALU.mult)
                ins.then_inc(y_rdy, 1)
            elif kind == "S":
                g, j = a // HPG, a % HPG
                dve.wait_ge(s_ps, a + 1)
                if j == 0:
                    dve.wait_ge(bias_in, (16, 32, 48)[g])
                if j == 0 and g == 2:
                    dve.wait_ge(att_st[0], 16)
                if a >= 2:
                    dve.wait_ge(p_sb, a - 1)
                ssb, og = Ssb[a % 2], Og[0 if g == 0 else 1]
                if g == 0:
                    pv = ps[:, 2:4, :].rearrange("p b (t k) -> p (b t) k", k=256)
                    dve.scalar_tensor_tensor(out=ssb[:, 1:4, :], in0=pv[:, 1:4, :], scalar=DH ** -0.5,
                                             in1=bc(bias[:, j, :], 1, 3), op0=ALU.mult, op1=ALU.add)
                    link(dve.scalar_tensor_tensor(out=ssb[:, 0, P:256], in0=pv[:, 0, P:256], scalar=DH ** -0.5,
                                                  in1=bias[:, j, P:256], op0=ALU.mult, op1=ALU.add))
                    dve.tensor_reduce(og[:, 1:4, j, DH:DH + 1], ssb[:, 1:4, :], AX.X, ALU.max)
                    link(dve.tensor_reduce(og[:, 0, j, DH:DH + 1], ssb[:, 0, P:256], AX.X, ALU.max))
                else:
                    link(dve.scalar_tensor_tensor(out=ssb[:, :, 0:P], in0=bank(2).rearrange("p (t k) -> p t k", k=P),
                                                  scalar=DH ** -0.5, in1=bc(bias[:, j, 0:P], 1, NT),
                                                  op0=ALU.mult, op1=ALU.add))
                    link(dve.tensor_reduce(og[:, :, j, DH:DH + 1], ssb[:, :, 0:P], AX.X, ALU.max))
                dve.tensor_scalar(nmx[a % 2], og[:, :, j, DH], -1.0, None, ALU.mult).then_inc(s_sb, 1)
            elif kind == "T":
                g = a // HPG
                dve.wait_ge(pt_ps, a + 1)
                if a >= 2:
                    dve.wait_ge(pv_ps, a - 1)
                if g == 0:
                    pv = ps[:, 4:6, :].rearrange("p b (m k) -> p (b m) k", k=P)
                    dve.tensor_copy(PT[a % 2][:, 1:8, :], pv[:, 1:8, :]).then_inc(pt_sb, 1)
                else:
                    dve.tensor_copy(PT[a % 2][:, 0:4, :], bank(4).rearrange("p (m k) -> p m k", k=P)).then_inc(pt_sb, 1)
            elif kind == "ada":
                if a == 4:
                    dve.wait_ge(zero_rdy, 2)
                ada_sum_up(a)
                ada_move(a)
            elif kind == "combine":
                dve.wait_ge(att_ld, 32)
                dve.wait_ge(og_rdy, 3 * HPG)
                O = [Og[0], O1, O2]
                f = [o[:, :, :, :].rearrange("p t h e -> p (t h) e") for o in O]
                link(dve.tensor_tensor(cmb[:, 3, :], f[0][:, :, DH], f[1][:, :, DH], ALU.max))
                link(dve.tensor_tensor(cmb[:, 3, :], cmb[:, 3, :], f[2][:, :, DH], ALU.max))
                for g in range(3):
                    ins = dve.tensor_tensor(cmb[:, g, :], f[g][:, :, DH], cmb[:, 3, :], ALU.subtract)
                ins.then_inc(cm_m, 1)
                dve.wait_ge(cm_e, 1)
                for g in range(3):
                    link(dve.tensor_tensor(cmb[:, 4 + g, :], cmb[:, g, :], f[g][:, :, DH + 1], ALU.mult))
                link(dve.tensor_tensor(cmb[:, 4, :], cmb[:, 4, :], cmb[:, 5, :], ALU.add))
                link(dve.tensor_tensor(cmb[:, 4, :], cmb[:, 4, :], cmb[:, 6, :], ALU.add))
                link(dve.reciprocal(cmb[:, 4, :], cmb[:, 4, :]))
                for g in range(3):
                    link(dve.tensor_tensor(cmb[:, g, :], cmb[:, g, :], cmb[:, 4, :], ALU.mult))
                yv = yatt[:, :, :, :].rearrange("p t h e -> p (t h) e")
                link(dve.tensor_tensor(yv, f[0][:, :, 0:DH], bc(cmb[:, 0, :], 2, DH), ALU.mult))
                for g in (1, 2):
                    link(dve.tensor_tensor(f[g][:, :, 0:DH], f[g][:, :, 0:DH], bc(cmb[:, g, :], 2, DH), ALU.mult))
                    link(dve.tensor_tensor(yv, yv, f[g][:, :, 0:DH], ALU.add))
                dve.sem_inc(yatt_rdy, 1)

        dve.wait_ge(lg_ps, 1)
        lgv = bank(4)[:, 0:64 * NT].rearrange("p (t n) -> p t n", n=64)
        gl = rt_w[:, 0:16].rearrange("p (t g) -> p t g", g=EG)
        el, elm = rt[:, 1, :, :], rt[:, 2, :, :]
        tmp, A = rt[:, 3, :, :], rt[:, 0, :, :]
        red = rt_w[:, 16:20]
        oh_g = rt_w[:, 48:64].rearrange("p (t g) -> p t g", g=EG)
        gsum, v1, v2, w1, w2 = (rt_w[:, n:n + 4] for n in (20, 24, 28, 36, 40))

        def first_max(v, onehot, vmax, rank, n, scratch):
            link(dve.tensor_reduce(vmax, v, AX.X, ALU.max))
            link(dve.tensor_tensor(scratch, v, bc(vmax, 2, n), ALU.is_equal))
            link(dve.tensor_tensor(scratch, scratch, bc(rank, 1, NT), ALU.mult))
            link(dve.tensor_reduce(red, scratch, AX.X, ALU.max))
            link(dve.tensor_tensor(onehot, scratch, bc(red, 2, n), ALU.is_equal))

        link(dve.tensor_tensor(gl, lgv[:, :, 0:EG], bc(brt[:, 0:EG], 1, NT), ALU.add))
        link(dve.tensor_tensor(el, lgv[:, :, EG:EG + NE], bc(brt[:, EG:EG + NE], 1, NT), ALU.add))
        g4 = rt[:, 4, 0, 0:16].rearrange("p (t g) -> p t g", g=EG)
        first_max(gl, oh_g, v1, cst[:, FIRST4:FIRST4 + EG], EG, g4)
        dve.tensor_tensor(gl, gl, bc(v1, 2, EG), ALU.subtract).then_inc(rt_ge, 1)
        link(dve.tensor_scalar(oh_g, oh_g, 1.0, -MASKED, ALU.subtract, ALU.mult))
        link(dve.tensor_tensor(elm.rearrange("p t (g e) -> p t g e", g=EG), el.rearrange("p t (g e) -> p t g e", g=EG),
                               bc(oh_g, 3, EPG), ALU.add))
        m1, m2 = rt_mask[:, 0, :, :], rt_mask[:, 1, :, :]
        dve.wait_ge(rt_gexp, 1)
        link(dve.tensor_reduce(gsum, gl, AX.X, ALU.add))
        first_max(elm, m1, v1, cst[:, FIRST32:FIRST32 + NE], NE, tmp)
        link(dve.scalar_tensor_tensor(out=elm, in0=m1, scalar=3.0 * MASKED, in1=elm, op0=ALU.mult, op1=ALU.add))
        first_max(elm, m2, v2, cst[:, FIRST32:FIRST32 + NE], NE, tmp)
        dve.tensor_tensor(A, m1, m2, ALU.add).then_inc(rt_asg, 1)
        dve.tensor_tensor(rt_w[:, 32:36], v2, v1, ALU.subtract).then_inc(rt_ge, 1)
        dve.wait_ge(rt_gexp, 2)
        ex = rt_w[:, 32:36]
        link(dve.tensor_scalar(w1, ex, 1.0, None, ALU.add))
        link(dve.tensor_tensor(w1, w1, gsum, ALU.mult))
        link(dve.reciprocal(w1, w1))
        link(dve.tensor_tensor(w2, w1, ex, ALU.mult))
        dve.tensor_copy(slot_w[:, 0:4], w1)
        dve.tensor_copy(slot_w[:, 4:8], w2)
        dve.wait_ge(rk_ps, 1)
        cnt, xe, inc, xb, tm = (rt[:, n, 0, :] for n in (4, 5, 6, 7, 8))
        link(dve.tensor_copy(cnt, bank(5)[:, NE * NT:NE * NT + NE]))
        link(dve.tensor_scalar(xe, cnt, float(C), None, ALU.is_gt))
        for m in (2, 3):
            link(dve.tensor_scalar(tm, cnt, float(m * C), None, ALU.is_gt))
            link(dve.tensor_tensor(xe, xe, tm, ALU.add))
        link(dve.tensor_tensor_scan(inc, ones[:, 0:NE], xe, 0.0, ALU.mult, ALU.add))
        link(dve.tensor_tensor(xb, inc, xe, ALU.subtract))
        link(dve.tensor_scalar(xb, xb, float(NE - 1), float(C), ALU.add, ALU.mult))
        link(dve.tensor_tensor(xb, xb, cst[:, E128:E128 + NE], ALU.subtract))
        rk = bank(5)[:, 0:NE * NT].rearrange("p (t n) -> p t n", n=NE)
        link(dve.tensor_scalar(tmp, rk, float(C), None, ALU.is_ge))
        link(dve.tensor_tensor(tmp, tmp, bc(xb, 1, NT), ALU.mult))
        link(dve.tensor_tensor(tmp, tmp, bc(cst[:, E128:E128 + NE], 1, NT), ALU.add))
        link(dve.tensor_tensor(tmp, tmp, rk, ALU.add))
        for k, m in enumerate((m1, m2)):
            link(dve.tensor_tensor(el, tmp, m, ALU.mult))
            link(dve.tensor_reduce(rt_w[:, 48 + 4 * k:52 + 4 * k], el, AX.X, ALU.add))
        link(dve.tensor_copy(slot_u, rt_w[:, 48:56]))
        dve.sem_inc(slot_rdy, 1)
        link(dve.tensor_copy(ctab_f[:, 0:NE], cst[:, I32:I32 + NE]))
        le = rt[:, 2:4, :, :].rearrange("p a t n -> p (a t) n")
        link(dve.tensor_tensor(le, bc(inc, 1, 8), bc(cst[:, J8:J8 + 8], 2, NE), ALU.is_le))
        link(dve.tensor_reduce(ctab_f[:, NE:NE + 8], le, AX.X, ALU.add))
        link(dve.tensor_scalar(ctab_f[:, NE:NE + 8], ctab_f[:, NE:NE + 8], float(NE - 1), None, ALU.min))
        link(dve.tensor_scalar(tm[:, 0:4], cst[:, EVEN:EVEN + 4], inc[:, NE - 1:NE], None, ALU.is_lt))
        link(dve.tensor_reduce(ctab_f[:, NCHUNK:NCHUNK + 1], tm[:, 0:4], AX.X, ALU.add))
        link(dve.tensor_scalar(ctab_f[:, NCHUNK:NCHUNK + 1], ctab_f[:, NCHUNK:NCHUNK + 1], float(NE // 2), None, ALU.add))
        link(dve.memset(ctab_f[:, NCHUNK - 1:NCHUNK], 0.0))
        link(dve.tensor_scalar(ctab_f[:, NCHUNK + 1:NCHUNK + 2], ctab_f[:, NCHUNK:NCHUNK + 1], -1.0, None, ALU.add))
        link(dve.tensor_copy(tab_u[:, 0:NCHUNK + 2], ctab_f[:, 0:NCHUNK + 2]))
        dve.sem_inc(tab_rdy, 1)
        dve.wait_ge(ids_ps, 1)
        dve.tensor_copy(idx_u[:, 0:NCHUNK], bank(6)[:, 0:NCHUNK]).then_inc(idx_rdy, 1)

        def w_rest(raw, hi, lo, n, by_columns=False):
            for h in range(2):
                v = (slice(None), slice(None), slice(512 * h, 512 * h + 512)) if by_columns else \
                    (slice(None), slice(4 * h, 4 * h + 4), slice(None))
                dve.wait_ge(m_hi, n + h + 1)
                dve.tensor_tensor(lo[v], raw[v], hi[v].bitcast(f32), ALU.subtract).then_inc(m_lo, 1)

        def x_rest(c):
            dve.wait_ge(x_hi, c + 1)
            dve.tensor_tensor(xT_lo[:, :, :], ps[:, 2:4, :].rearrange("p b (k c) -> p (b k) c", c=C),
                              xT_hi[:, :, :].bitcast(f32), ALU.subtract).then_inc(m_xT, 1)

        def chunk(i, s):
            c = 2 * i + s
            w_rest(wu, wu_hi, wu_lo, 6 * c + 2)
            dve.wait_ge(m_sig, c + 1)
            wait(dve, m_h, c)
            dve.tensor_tensor(gsb[:, :], bank(0), sgb[:, :], ALU.mult).then_inc(m_gs, 1)
            w_rest(wd, wd_hi, wd_lo, 6 * c + 4, by_columns=True)
            dve.wait_ge(m_up, c + 1)
            dve.wait_ge(m_gs, c + 1)
            wait(dve, m_hps, c)
            dve.tensor_tensor(hb[:, :], bank(1), gsb[:, :], ALU.mult).then_inc(m_h, 1)
            dve.wait_ge(h_hi, c + 1)
            dve.tensor_tensor(hT_lo[:, :, :], bank(4).rearrange("p (f c) -> p f c", c=C),
                              hT_hi[:, :, :].bitcast(f32), ALU.subtract).then_inc(m_hT, 1)
            x_rest(c + 1)
            w_rest(wg[1 - s], wg_hi[1 - s], wg_lo[1 - s], 6 * c + 6)

        dve.wait_ge(tab_rdy, 1)
        w_rest(wg[0], wg_hi[0], wg_lo[0], 0)
        x_rest(0)
        chunk(0, 0)
        chunk(0, 1)
        with dve.Fori(1, pair_count(dve)) as i:
            chunk(i, 0)
            chunk(i, 1)
        dve.wait_ge(ln2_in, 32)
        dve.wait_ge(x1_back, 16)
        for t in range(NT):
            s = t % 2
            dve.wait_ge(fin_in[s], 32 * (t // 2 + 1))
            if t >= 2:
                dve.wait_ge(out_st[s], 16 * (t // 2))
            a, b, r = ya[s][:, :], yc[s][:, :], r2[s][:, :]
            link(dve.tensor_scalar(a, a, slot_w[:, t:t + 1], None, ALU.mult))
            link(dve.scalar_tensor_tensor(out=a, in0=b, scalar=slot_w[:, NT + t:NT + t + 1], in1=a, op0=ALU.mult, op1=ALU.add))
            link(dve.tensor_tensor(a, a, mods[:, 3, :], ALU.mult))
            link(dve.scalar_tensor_tensor(out=r, in0=x1[:, t, :], scalar=ALPHA, in1=a, op0=ALU.mult, op1=ALU.add))
            dve.sem_inc(fin_use, 1)
            norm_rows(r, ln2gb[:, 0, :], ln2gb[:, 1, :])
            dve.sem_inc(fin_rdy, 1)

    ctx.close()


def kernel(x, c, rel_bias, w_ada, b_ada, w_in, w_gla_gate, b_gla_gate, gla_norm, w_proj_gla, w_proj_attn,
           w_out, ln1_g, ln1_b, w_router_group, b_router_group, w_router_expert, b_router_expert,
           w_exp_gate, w_exp_up, w_exp_down, ln2_g, ln2_b):
    import concourse.bacc as bacc
    from concourse.bass_utils import run_bass_kernel_spmd

    def a(v):
        return np.ascontiguousarray(np.asarray(v))

    feeds = [
        a(x[0]), a(np.asarray(c).reshape(KD, P).T), a(rel_bias), a(w_ada[0]), a(b_ada), a(w_in[0]), a(w_gla_gate[0]),
        a(np.asarray(b_gla_gate).reshape(GH, GDK).T), a(gla_norm), a(w_proj_gla[0]), a(w_proj_attn[0]), a(w_out[0]),
        a(ln1_g), a(ln1_b),
        a(np.concatenate([np.asarray(w_router_group[0]), np.asarray(w_router_expert[0])], axis=1)),
        a(np.concatenate([np.asarray(b_router_group[0]), np.asarray(b_router_expert[0])])),
        a(w_exp_gate[0]).reshape(NE, D, FF), a(w_exp_up[0]).reshape(NE, D, FF), a(w_exp_down[0]).reshape(NE, FF, D),
        a(ln2_g), a(ln2_b), shape_constants(), bias_selectors(),
    ]
    nc = bacc.Bacc("TRN2", target_bir_lowering=False, num_devices=1)
    arrays, args = {}, []
    for n, v in enumerate(feeds):
        arrays[f"in{n}"] = v
        args.append(nc.dram_tensor(f"in{n}", v.shape, mybir.dt.from_np(v.dtype), kind="ExternalInput").ap())
    out = nc.dram_tensor("out", (S, D), mybir.dt.float32, kind="ExternalOutput").ap()
    build(nc, *args, out)
    r = run_bass_kernel_spmd(nc, [arrays], core_ids=[0])
    return r.results[0]["out"].reshape(1, S, D)
```
